# Optimizing a Trainium2 kernel written in Bass

```python
import jax
import jax.numpy as jnp
from jax import lax
import numpy as np

D_MODEL = 1024
BATCH = 1
SEQ = 256
DEPTH = 2

GRID_W = 64
CTX_LEN = 256
N_EVEN = (DEPTH + 1) // 2
N_ODD = DEPTH // 2
N_MOD = 9
D_FF = 2816
D_POOL = D_MODEL // 4
POOL_WINDOWS = (2, 4, 8, 16)
N_POOL_GROUPS = len(POOL_WINDOWS)
POOL_GROUP_DIM = D_POOL // N_POOL_GROUPS
D_HGRN = D_MODEL - D_POOL
HGRN_HEAD_DIM = 128
N_HGRN_HEADS = D_HGRN // HGRN_HEAD_DIM
HGRN_CHUNK = 64
D_IN_AB = D_POOL + 5 * D_HGRN
D_GMLP = D_MODEL
GMLP_CHUNK = 128
GMLP_GROUP_DIM = 128
N_GMLP_GROUPS = D_GMLP // GMLP_GROUP_DIM
EPS = 1e-6

kernel_name = 'hybrid_pool_hgrn2_gmlp_macaron_dit'

def rms_norm(x, g):
    xf = x.astype(jnp.float32)
    y = xf * lax.rsqrt(jnp.mean(xf * xf, axis=-1, keepdims=True) + EPS)
    return (y * g.astype(jnp.float32)).astype(x.dtype)

def layer_norm(x, g, b):
    xf = x.astype(jnp.float32)
    xc = xf - jnp.mean(xf, axis=-1, keepdims=True)
    y = xc * lax.rsqrt(jnp.mean(xc * xc, axis=-1, keepdims=True) + EPS)
    return (y * g.astype(jnp.float32) + b.astype(jnp.float32)).astype(x.dtype)

def adaln(x, g, mod, s):
    return rms_norm(x, g) * (1 + mod[:, :, 3 * s + 1]) + mod[:, :, 3 * s]

def gate_of(mod, s):
    return mod[:, :, 3 * s + 2]

def swiglu(h, w1, w3, w2):
    return (jax.nn.silu(h @ w1) * (h @ w3)) @ w2

def centred_mean(x, w):
    L = x.shape[-2]
    cs = jnp.cumsum(x.astype(jnp.float32), axis=-2)
    cs = jnp.concatenate([jnp.zeros_like(cs[..., :1, :]), cs], axis=-2)
    t = jnp.arange(L)
    lo = jnp.clip(t - w // 2, 0, L)
    hi = jnp.clip(t - w // 2 + w, 0, L)
    total = jnp.take(cs, hi, axis=-2) - jnp.take(cs, lo, axis=-2)
    count = (hi - lo).astype(jnp.float32)[:, None]
    return (total / count).astype(x.dtype)

def pool_mixer(xa, w_pool, scale, on_grid):
    B, L, _ = xa.shape
    if on_grid:
        rows = L // GRID_W
        xr = xa.reshape(B, rows, GRID_W, D_POOL)
    else:
        xr = xa
    groups = jnp.split(xr, N_POOL_GROUPS, axis=-1)
    y = jnp.stack([centred_mean(g, w) - g for g, w in zip(groups, POOL_WINDOWS)], axis=-2)
    y = jnp.einsum('...gc,gcd->...gd', y, w_pool)
    return y.reshape(B, L, D_POOL) * scale

def split_heads(a):
    B, L, _ = a.shape
    return a.reshape(B, L, N_HGRN_HEADS, HGRN_HEAD_DIM).transpose(0, 2, 1, 3).astype(jnp.float32)

def hgrn_prep(p, lb):
    q, v, f_fwd, f_bwd, g = jnp.split(p, 5, axis=-1)
    q = split_heads(jax.nn.silu(q)) * (HGRN_HEAD_DIM ** -0.5)
    v = split_heads(v)
    dirs = []
    for f, lbd in ((f_fwd, lb[0]), (f_bwd, lb[1])):
        lbh = lbd.astype(jnp.float32).reshape(1, N_HGRN_HEADS, 1, HGRN_HEAD_DIM)
        forget = lbh + (1 - lbh) * jax.nn.sigmoid(split_heads(f))
        dirs.append((1 - forget, jnp.log(forget)))
    return q, v, dirs, g

def hgrn_chunk_scan(q, k, v, logf, s0):
    B, H, L, _ = q.shape
    n = L // HGRN_CHUNK

    def to_chunks(a):
        return jnp.moveaxis(a.reshape(B, H, n, HGRN_CHUNK, a.shape[-1]), 2, 0)

    mask = jnp.tril(jnp.ones((HGRN_CHUNK, HGRN_CHUNK), dtype=bool))[:, :, None]

    def step(S, inp):
        qc, kc, vc, lf = inp
        b = jnp.cumsum(lf, axis=2)
        o_inter = jnp.einsum('bhjk,bhkv->bhjv', qc * jnp.exp(b), S)
        diff = b[:, :, :, None, :] - b[:, :, None, :, :]
        decay = jnp.exp(jnp.where(mask, diff, -jnp.inf))
        a = jnp.einsum('bhjk,bhjik,bhik->bhji', qc, decay, kc)
        o = o_inter + jnp.einsum('bhji,bhiv->bhjv', a, vc)
        b_last = b[:, :, -1:, :]
        S = jnp.exp(b[:, :, -1, :])[..., None] * S + jnp.einsum('bhik,bhiv->bhkv', kc * jnp.exp(b_last - b), vc)
        return S, o

    S, o = lax.scan(step, s0, (to_chunks(q), to_chunks(k), to_chunks(v), to_chunks(logf)))
    o = jnp.moveaxis(o, 0, 2).reshape(B, H, L, v.shape[-1])
    return o, S

def hgrn_readout(o, gate, g_norm, dtype):
    B, H, L, dv = o.shape
    o = o.transpose(0, 2, 1, 3)
    o = o * lax.rsqrt(jnp.mean(o * o, axis=-1, keepdims=True) + EPS)
    o = o.reshape(B, L, D_HGRN) * g_norm.astype(jnp.float32)
    return (o * jax.nn.silu(gate.astype(jnp.float32))).astype(dtype)

def hgrn_mixer(p_lat, p_ctx, lb, g_norm):
    q_l, v_l, dirs_l, gate_l = hgrn_prep(p_lat, lb)
    q_c, v_c, dirs_c, gate_c = hgrn_prep(p_ctx, lb)
    B = p_lat.shape[0]
    s0 = jnp.zeros((B, N_HGRN_HEADS, HGRN_HEAD_DIM, HGRN_HEAD_DIM), jnp.float32)
    o_lat = jnp.zeros_like(v_l)
    o_ctx = jnp.zeros_like(v_c)
    for d, reverse in enumerate((False, True)):
        def flip(a, reverse=reverse):
            return jnp.flip(a, axis=2) if reverse else a
        k_c, lf_c = dirs_c[d]
        k_l, lf_l = dirs_l[d]
        oc, s_ctx = hgrn_chunk_scan(flip(q_c), flip(k_c), flip(v_c), flip(lf_c), s0)
        ol, _ = hgrn_chunk_scan(flip(q_l), flip(k_l), flip(v_l), flip(lf_l), s_ctx)
        o_ctx = o_ctx + flip(oc)
        o_lat = o_lat + flip(ol)
    return (hgrn_readout(o_lat, gate_l, g_norm, p_lat.dtype),
            hgrn_readout(o_ctx, gate_c, g_norm, p_ctx.dtype))

def ab_mixer(h_lat, h_ctx, w_in, w_pool, pool_scale, lb, g_norm, w_out):
    p_lat = h_lat @ w_in
    p_ctx = h_ctx @ w_in
    a_lat = pool_mixer(p_lat[..., :D_POOL], w_pool, pool_scale, True)
    a_ctx = pool_mixer(p_ctx[..., :D_POOL], w_pool, pool_scale, False)
    b_lat, b_ctx = hgrn_mixer(p_lat[..., D_POOL:], p_ctx[..., D_POOL:], lb, g_norm)
    out_lat = jnp.concatenate([a_lat, b_lat], axis=-1) @ w_out
    out_ctx = jnp.concatenate([a_ctx, b_ctx], axis=-1) @ w_out
    return out_lat, out_ctx

def gmlp_mixer(h, w_in, ln_g, ln_b, w_s, b_s, w_out):
    B, L, _ = h.shape
    z = jax.nn.gelu(h @ w_in)
    u, v = jnp.split(z, 2, axis=-1)
    v = layer_norm(v, ln_g, ln_b)
    n = L // GMLP_CHUNK
    vr = v.reshape(B, n, GMLP_CHUNK, N_GMLP_GROUPS, GMLP_GROUP_DIM)
    sv = jnp.einsum('gpq,bnqgc->bnpgc', w_s, vr) + b_s.T[None, None, :, :, None]
    return (u * sv.reshape(B, L, D_GMLP)) @ w_out

def setup_inputs(seed: int = 0) -> dict:
    key = jax.random.key(seed)
    ks = jax.random.split(key, 23)
    D = D_MODEL

    def nrm(k, shape, scale):
        return jax.random.normal(k, shape, jnp.float32) * scale

    return {
        'x': nrm(ks[0], (BATCH, SEQ, D), 1.0),
        'c': nrm(ks[1], (BATCH, D), 1.0),
        'ctx': nrm(ks[2], (BATCH, CTX_LEN, D), 1.0),
        'c_ctx': nrm(ks[3], (D,), 1.0),
        'mod_w': nrm(ks[4], (DEPTH, D, N_MOD * D), 0.5 * D ** -0.5),
        'mod_b': nrm(ks[5], (DEPTH, N_MOD * D), 0.02),
        'norm_g': 1.0 + nrm(ks[6], (DEPTH, 3, D), 0.05),
        'ffn_w1': nrm(ks[7], (DEPTH, 2, D, D_FF), D ** -0.5),
        'ffn_w3': nrm(ks[8], (DEPTH, 2, D, D_FF), D ** -0.5),
        'ffn_w2': nrm(ks[9], (DEPTH, 2, D_FF, D), D_FF ** -0.5),
        'ab_w_in': nrm(ks[10], (N_EVEN, D, D_IN_AB), D ** -0.5),
        'pool_w': nrm(ks[11], (N_EVEN, N_POOL_GROUPS, POOL_GROUP_DIM, POOL_GROUP_DIM), POOL_GROUP_DIM ** -0.5),
        'pool_scale': 1.0 + nrm(ks[12], (N_EVEN, D_POOL), 0.05),
        'hgrn_lb': nrm(ks[13], (N_EVEN + 1, 2, D_HGRN), 1.0),
        'hgrn_norm_g': 1.0 + nrm(ks[14], (N_EVEN, D_HGRN), 0.05),
        'ab_w_out': nrm(ks[15], (N_EVEN, D_POOL + D_HGRN, D), (D_POOL + D_HGRN) ** -0.5),
        'gmlp_w_in': nrm(ks[16], (N_ODD, D, 2 * D_GMLP), D ** -0.5),
        'gmlp_ln_g': 1.0 + nrm(ks[17], (N_ODD, D_GMLP), 0.05),
        'gmlp_ln_b': nrm(ks[18], (N_ODD, D_GMLP), 0.02),
        'gmlp_w_s': nrm(ks[19], (N_ODD, N_GMLP_GROUPS, GMLP_CHUNK, GMLP_CHUNK), GMLP_CHUNK ** -0.5),
        'gmlp_b_s': 1.0 + nrm(ks[20], (N_ODD, N_GMLP_GROUPS, GMLP_CHUNK), 0.05),
        'gmlp_w_out': nrm(ks[21], (N_ODD, D_GMLP, D), D_GMLP ** -0.5),
        'final_g': 1.0 + nrm(ks[22], (D,), 0.05),
    }

def reference(x, c, ctx, c_ctx, mod_w, mod_b, norm_g, ffn_w1, ffn_w3, ffn_w2,
              ab_w_in, pool_w, pool_scale, hgrn_lb, hgrn_norm_g, ab_w_out,
              gmlp_w_in, gmlp_ln_g, gmlp_ln_b, gmlp_w_s, gmlp_b_s, gmlp_w_out, final_g):
    B = x.shape[0]
    lb_all = jnp.cumsum(jax.nn.softmax(hgrn_lb.astype(jnp.float32), axis=0), axis=0)
    xl, xc = x, ctx
    for i in range(DEPTH):
        ctx_live = any(j % 2 == 0 for j in range(i, DEPTH))
        mod_l = (jax.nn.silu(c) @ mod_w[i] + mod_b[i]).reshape(B, 1, N_MOD, D_MODEL)
        mod_c = (jax.nn.silu(c_ctx) @ mod_w[i] + mod_b[i]).reshape(1, 1, N_MOD, D_MODEL)

        xl = xl + 0.5 * gate_of(mod_l, 0) * swiglu(adaln(xl, norm_g[i, 0], mod_l, 0), ffn_w1[i, 0], ffn_w3[i, 0], ffn_w2[i, 0])
        if ctx_live:
            xc = xc + 0.5 * gate_of(mod_c, 0) * swiglu(adaln(xc, norm_g[i, 0], mod_c, 0), ffn_w1[i, 0], ffn_w3[i, 0], ffn_w2[i, 0])

        h_l = adaln(xl, norm_g[i, 1], mod_l, 1)
        if i % 2 == 0:
            e = i // 2
            h_c = adaln(xc, norm_g[i, 1], mod_c, 1)
            o_l, o_c = ab_mixer(h_l, h_c, ab_w_in[e], pool_w[e], pool_scale[e], lb_all[e], hgrn_norm_g[e], ab_w_out[e])
            xc = xc + gate_of(mod_c, 1) * o_c
        else:
            o = i // 2
            o_l = gmlp_mixer(h_l, gmlp_w_in[o], gmlp_ln_g[o], gmlp_ln_b[o], gmlp_w_s[o], gmlp_b_s[o], gmlp_w_out[o])
            if ctx_live:
                h_c = adaln(xc, norm_g[i, 1], mod_c, 1)
                o_c = gmlp_mixer(h_c, gmlp_w_in[o], gmlp_ln_g[o], gmlp_ln_b[o], gmlp_w_s[o], gmlp_b_s[o], gmlp_w_out[o])
                xc = xc + gate_of(mod_c, 1) * o_c
        xl = xl + gate_of(mod_l, 1) * o_l

        xl = xl + 0.5 * gate_of(mod_l, 2) * swiglu(adaln(xl, norm_g[i, 2], mod_l, 2), ffn_w1[i, 1], ffn_w3[i, 1], ffn_w2[i, 1])
        if ctx_live:
            xc = xc + 0.5 * gate_of(mod_c, 2) * swiglu(adaln(xc, norm_g[i, 2], mod_c, 2), ffn_w1[i, 1], ffn_w3[i, 1], ffn_w2[i, 1])
    return rms_norm(xl, final_g)


_drawn_inputs = setup_inputs


def setup_inputs(seed=0):
    import zlib

    import numpy as np

    out = dict(_drawn_inputs(seed))
    spreads = {}
    factors = {'ctx': 7.239,
     'c_ctx': 7.534,
     'pool_scale': 8.0,
     'hgrn_lb': 4.617,
     'hgrn_norm_g': 6.335,
     'gmlp_ln_g': 5.536,
     'gmlp_ln_b': 34.142,
     'gmlp_b_s': 5.619}
    for name, (base, spread) in spreads.items():
        noise = np.random.default_rng([zlib.crc32(name.encode()), seed]).standard_normal(out[name].shape)
        drawn = base * np.exp(spread * noise) if base else spread * noise
        out[name] = jnp.asarray(drawn.astype(out[name].dtype))
    for name, factor in factors.items():
        out[name] = (out[name] * factor).astype(out[name].dtype)
    return out
```

```python
from contextlib import ExitStack

import numpy as np

import concourse.bass as bass
from concourse import mybir

F32 = mybir.dt.float32
F32R = mybir.dt.float32r
U8 = mybir.dt.uint8
ALU = mybir.AluOpType
ACT = mybir.ActivationFunctionType
AX = mybir.AxisListType

P = 128
D = 1024
KC = D // P
LAT = 256
CTX = 256
BOTH = LAT + CTX
FF = 2816
NF = FF // P
NF_FIRST = 12
POOL_TILES = 2
HEADS = 6
DH = 128
D_HGRN = HEADS * DH
GRID_W = 64
PAD = 8
ROWS = LAT // GRID_W
RW = GRID_W + 2 * PAD
N_MOD = 9
GROUPS = 8
EPS = 1e-6
LEVELS = 8
SLOTS = 4

C_NORM, C_FINAL, C_LB, C_HG, C_PS, C_C, C_CC, N_PAR = 0, 48, 56, 80, 86, 88, 96, 104


class Step:

    def __init__(self, kind, layer, pA, pB, pEnd):
        self.kind, self.layer, self.pA, self.pB, self.pEnd = kind, layer, pA, pB, pEnd


def plan():
    steps, p, q = [], 0, 0

    def ffn(layer, j, T, f0, nf):
        nonlocal p, q
        s = Step("ffn", layer, p, p + nf, p + nf + nf // 2)
        s.j, s.T, s.f0, s.nf, s.q0 = j, T, f0, nf, q
        p += nf + nf // 2
        q += nf
        steps.append(s)

    def mix(kind, layer, n_in, n_out):
        nonlocal p
        steps.append(Step(kind, layer, p, p + n_in, p + n_in + n_out))
        p += n_in + n_out

    ffn(0, 0, BOTH, 0, NF_FIRST)
    ffn(0, 0, BOTH, NF_FIRST, NF - NF_FIRST)
    mix("ab", 0, 16, 4)
    ffn(0, 1, LAT, 0, NF)
    ffn(1, 0, LAT, 0, NF)
    mix("gmlp", 1, 8, 4)
    ffn(1, 1, LAT, 0, NF)
    return steps, p


STEPS, N_PAIRS = plan()
N_TILES = 2 * N_PAIRS

JOBS = [(0, v, m) for m in (2, 3, 4) for v in (0, 1)] + [(0, 0, m) for m in range(5, 9)] \
    + [(1, 0, m) for m in range(9)]
JOBS_AT = {0: ((4, (0, 1)), (10, (2, 3))), 1: ((2, (4, 5)), (8, (6, 7))), 3: ((8, (10, 11)), (20, (12, 13))),
           4: ((8, (14, 15)), (20, (16, 17))), 6: ((8, (18,)),)}
JOBS_AT_AB = (8, 9)


def build(nc, t):
    stack = ExitStack()
    with stack:
        _build(nc, t, stack)


def _build(nc, t, stack):
    def sb(name, shape, dt=F32, within=stack):
        return within.enter_context(nc.sbuf_tensor(name, shape, dt))

    xT = sb("xT", [P, KC, BOTH])
    xn_hi = sb("xn_hi", [P, KC, BOTH], F32R)
    xn_lo = sb("xn_lo", [P, KC, BOTH], F32R)
    w_raw = sb("w_raw", [P, SLOTS, D])
    w_hi = sb("w_hi", [P, SLOTS, D], F32R)
    w_lo = sb("w_lo", [P, SLOTS, D], F32R)
    m_raw = sb("m_raw", [P, 2, 2, D])
    m_acc = sb("m_acc", [P, 2, D])
    rms = sb("rms", [P, BOTH])
    rstd = sb("rstd", [P, BOTH])
    sq = sb("sq", [P, 2, BOTH])
    tbuf = sb("tbuf", [P, 3, LAT])
    act_s = sb("act_s", [P, 2, BOTH])
    hm = sb("hm", [P, 2, BOTH])
    ident = sb("ident", [P, P])
    ones = sb("ones", [P, P])
    masks = sb("masks", [P, LEVELS, P], U8)
    inv_cnt = sb("inv_cnt", [P, POOL_TILES, GRID_W])
    par_rows = sb("par_rows", [P, P])
    mb_rows = sb("mb_rows", [P, 2, P])
    par = sb("par", [P, N_PAR])
    mod_b = sb("mod_b", [P, 2, N_MOD * KC])
    mods = sb("mods", [P, 3, N_MOD * KC])
    silu_c = sb("silu_c", [P, 2 * KC])
    lb_t = sb("lb_t", [P, 4, 2 * HEADS])
    lb = sb("lb", [P, 2 * HEADS])
    one_lb = sb("one_lb", [P, 2 * HEADS])
    eps = sb("eps", [P, 1])
    stat = sb("stat", [P, 8])

    part = ExitStack()
    xin = sb("xin", [P, 4, D], within=part)
    m_first = sb("m_first", [P, 8, D], within=part)
    masks_in = sb("masks_in", [P, LEVELS, P], within=part)
    part.close()
    part = ExitStack()
    h_hi = sb("h_hi", [P, NF_FIRST * BOTH], F32R, within=part)
    h_lo = sb("h_lo", [P, NF_FIRST * BOTH], F32R, within=part)
    part.close()
    part = ExitStack()
    Fg = sb("Fg", [P, 2, BOTH], within=part)
    Fb = sb("Fb", [P, 2 * BOTH], within=part)
    Kd = sb("Kd", [P, 2, 2, BOTH], within=part)
    Qd = sb("Qd", [P, 2, 2, LAT], within=part)
    Vd = sb("Vd", [P, 2, 4, DH], within=part)
    Am = sb("Am", [P, 2, P], within=part)
    Ax = sb("Ax", [P, 2, P], within=part)
    kT = sb("kT", [P, 4, P], within=part)
    Sd = sb("Sd", [P, 2, DH], within=part)
    Gs = sb("Gs", [P, HEADS, LAT], within=part)
    Os = sb("Os", [P, HEADS, LAT], within=part)
    py = sb("py", [P, POOL_TILES, LAT], within=part)
    pw = sb("pw", [P, POOL_TILES, P], within=part)
    early = ExitStack()
    xp = sb("xp", [P, POOL_TILES, ROWS * RW], within=early)
    xs = sb("xs", [P, 2, ROWS * RW], within=early)
    early.close()
    Kc = sb("Kc", [P, LEVELS + 1, LAT], within=part)
    Qc = sb("Qc", [P, LEVELS + 1, LAT], within=part)
    part.close()
    osq, orms, orstd = rms[:, LAT:BOTH], rms[:, 0:LAT], rstd[:, 0:LAT]
    part = ExitStack()
    Ug = sb("Ug", [P, GROUPS, LAT], within=part)
    Vt = sb("Vt", [P, 2, D], within=part)
    ws = sb("ws", [P, GROUPS, P], within=part)
    wsT = sb("wsT", [P, GROUPS, P], within=part)
    ln_g = sb("ln_g", [P, D], within=part)
    ln_b = sb("ln_b", [P, D], within=part)
    bs = sb("bs", [P, D], within=part)
    sv = sb("sv", [P, 2, LAT], within=part)
    part.close()
    part = ExitStack()
    yT = sb("yT", [P, KC, LAT], within=part)
    yo = sb("yo", [P, 2, D], within=part)
    part.close()

    ps = stack.enter_context(nc.psum_tensor("ps", [P, 8, 512], F32))

    sem = {name: stack.enter_context(nc.semaphore(name)) for name in (
        "consts params xin_full m_first_full0 m_first_full1 pool_w gm_in "
        "raw_full0 raw_full1 raw_full2 raw_full3 hi_done lo_done tile_used "
        "m_full0 m_full1 pool_seq pool_held acc_done mod_red mod_fin first_red "
        "dve act pe_x x_upd sq_done sq_used rms_done rstd_done t_done xhi_done xn_done "
        "silu_done gated hhi_done hlo_done "
        "pool_in q_read sig_done f_done v_raw vt_done v_done kq0_done q_init gathered k_upd f_merged q_upd k_final q_final lvl_done cp_done "
        "kt_done kt_copied s_done s_copied o_done o_copied oss_done orms_done o_scaled py_done pm_done g_sig g_done "
        "u_done ln_a ln_d ws_t wsT_done sv_done y_done yt_done yo_done out_done"
    ).split()}
    raw_full = [sem["raw_full0"], sem["raw_full1"], sem["raw_full2"], sem["raw_full3"]]
    m_full = [sem["m_full0"], sem["m_full1"]]

    def tok(T):
        return slice(0, T)

    def y_at(T, d):
        if T == BOTH:
            return ps[:, 4 + d if d < 4 else d - 4, :]
        return ps[:, 4 + d // 2, LAT * (d % 2):LAT * (d % 2) + LAT]

    def ssq_bank(T):
        return 4 if T == BOTH else 0

    def mod_cols(layer, ctx, m):
        row = 2 if layer else ctx
        return mods[:, row, m * KC:(m + 1) * KC]

    def h_at(buf, T, f):
        return buf[:, f * T:(f + 1) * T] if isinstance(f, int) else buf[:, bass.ds(f * T, T)]

    def ap3(buf, width, offset, *dims):
        return bass.AP(buf, offset, [[width, P], *[list(d) for d in dims]])

    def picked_k(par_, B, lat_only, ctx_only=False):
        n, off = (LAT if lat_only or ctx_only else BOTH), par_ * 2 * BOTH + (LAT if ctx_only else 0)
        return ap3(Kd, 4 * BOTH, off, (2 * B, n // (2 * B)), (BOTH + B, 2), (1, B))

    def picked_q(par_, B):
        return ap3(Qd, 4 * LAT, par_ * 2 * LAT, (2 * B, LAT // (2 * B)), (LAT + B, 2), (1, B))

    def blocks(B):
        return (Fg, 2 * BOTH, 0) if B == 1 else (Fb, 2 * BOTH, block_at(B))

    def block_at(B):
        at, b = 0, 2
        while b < B:
            at += 2 * BOTH // b
            b *= 2
        return at

    def other_k(B, ctx_only=False):
        buf, width, at = blocks(B)
        n = BOTH // B
        pairs, skip = (CTX // (2 * B), LAT // B) if ctx_only else (n // 2, 0)
        return ap3(buf, width, at + skip + 1, (2, pairs), (n - 1, 2), (0, B))

    def other_q(B):
        buf, width, at = blocks(B)
        n = BOTH // B
        return ap3(buf, width, at + n + 1, (2, LAT // B // 2), (-n - 1, 2), (0, B))

    def as3(ap, B):
        return ap.rearrange("p (n two b) -> p n two b", two=2, b=B)

    def in_pairs(e, p0, n, body):
        done = 0
        if n >= 4:
            with e.Fori(0, n // 2) as i:
                body(i * 2, p0 % 2)
                body(i * 2 + 1, (p0 + 1) % 2)
            done = n // 2 * 2
        for l in range(done, n):
            body(l, (p0 + l) % 2)

    def with_jobs(e, si, first, body, take):
        s, at = STEPS[si], first
        for until, jobs in JOBS_AT[si] + ((s.nf, ()),):
            part_ = lambda l, parity, off=at: body(l + off, parity)
            in_pairs(e, s.pA + at, until - at, part_)
            take(jobs)
            at = until

    block = stack.enter_context(nc.Block())

    @block.sync
    def _(sp):
        sp.dma_start(ident[:, :], t["ident"]).then_inc(sem["consts"], 16)
        sp.dma_start(masks_in[:, :, :], t["masks"]).then_inc(sem["consts"], 16)
        sp.dma_start(inv_cnt[:, :, :], t["inv_cnt"]).then_inc(sem["consts"], 16)
        sp.dma_start(par_rows[0:N_PAR, :], t["params"]).then_inc(sem["params"], 16)
        sp.dma_start(mb_rows[0:N_MOD * KC, :, :], t["mod_b"].rearrange("l (r c) -> r l c", c=P)).then_inc(sem["params"], 16)
        sp.dma_start(xin[:, 0:2, :], t["x"].rearrange("(n p) d -> p n d", p=P)).then_inc(sem["xin_full"], 16)
        sp.dma_start(xin[:, 2:4, :], t["ctx"].rearrange("(n p) d -> p n d", p=P)).then_inc(sem["xin_full"], 16)
        first = t["mod_w"][0].rearrange("(k p) c -> p k c", p=P)
        for g in range(4):
            half = [sem["m_first_full0"], sem["m_first_full1"]][g % 2]
            if g >= 2:
                sp.wait_ge(sem["first_red"], g - 1)
            sp.dma_start(m_first[:, 4 * (g % 2):4 * (g % 2) + 4, :],
                         first[:, 4 * (g % 2):4 * (g % 2) + 4, (g // 2) * D:(g // 2 + 1) * D]).then_inc(half, 16)

        def load(n, slot, src, free=True):
            if free:
                sp.wait_ge(sem["hi_done"], n - (SLOTS - 1))
                sp.wait_ge(sem["lo_done"], n - (SLOTS - 1))
            dst = w_raw[:, slot, :]
            if len(src.shape) == 3:
                dst = dst.rearrange("p (k c) -> p k c", k=KC)
            sp.dma_start(dst, src).then_inc(raw_full[slot], 16)

        def cols(w, c):
            v = w.rearrange("(k p) c -> p k c", p=P)
            return v[:, :, c * P:(c + 1) * P] if isinstance(c, int) else v[:, :, bass.ds(c * P, P)]

        def rows(w, r):
            return w[r * P:(r + 1) * P, :] if isinstance(r, int) else w[bass.ds(r * P, P), :]

        for s in STEPS:
            if s.kind == "ffn":
                w1, w3, w2 = t["w1"][s.layer, s.j], t["w3"][s.layer, s.j], t["w2"][s.layer, s.j]

                def up(l, parity, skip=0):
                    for j, w in enumerate((w1, w3)):
                        load(2 * (s.pA + skip + l) + j, 2 * parity + j, cols(w, l + (s.f0 + skip)), free=skip or s.pA)

                def down(l, parity):
                    for j in range(2):
                        load(2 * (s.pB + l) + j, 2 * parity + j, rows(w2, l * 2 + (s.f0 + j)))

                if s.pA == 0:
                    up(0, 0)
                    up(1, 1)
                    in_pairs(sp, s.pA + 2, s.nf - 2, lambda l, parity: up(l, parity, 2))
                else:
                    in_pairs(sp, s.pA, s.nf, up)
                in_pairs(sp, s.pB, s.nf // 2, down)
            elif s.kind == "ab":
                tiles = [0, 1]
                q0, v0, f0, b0, g0 = (POOL_TILES + HEADS * i for i in range(5))
                for h in range(HEADS):
                    tiles += [f0 + h, b0 + h, q0 + h, v0 + h]
                tiles += [g0 + h for h in range(HEADS)]
                for i, c in enumerate(tiles):
                    load(2 * s.pA + i, (2 * s.pA + i) % SLOTS, cols(t["ab_w_in"], c))
                    if i == 1:
                        sp.wait_ge(sem["pool_w"], 1)
                        for g in range(4):
                            r = 64 * (g % 2)
                            sp.dma_start(pw[r:r + 64, g // 2, r:r + 64], t["pool_w"][g]).then_inc(sem["pool_w"], 16)
                for i in range(KC):
                    load(2 * s.pB + i, (2 * s.pB + i) % SLOTS, rows(t["ab_w_out"], i))
            else:
                sp.wait_ge(sem["tile_used"], 2 * s.pA + SLOTS)
                sp.dma_start(ws[:, :, :], t["gmlp_w_s"].rearrange("g p q -> p g q")).then_inc(sem["gm_in"], 16)
                for dst, src in ((ln_g, t["gmlp_ln_g"]), (ln_b, t["gmlp_ln_b"]), (bs, t["gmlp_b_s"])):
                    sp.dma_start(dst[:, :], src[None, :].to_broadcast((P, D))).then_inc(sem["gm_in"], 16)
                in_pairs(sp, s.pA, 8, lambda l, parity: [
                    load(2 * (s.pA + l) + j, 2 * parity + j, cols(t["gmlp_w_in"], l * 2 + j)) for j in range(2)])
                in_pairs(sp, s.pB, 4, lambda l, parity: [
                    load(2 * (s.pB + l) + j, 2 * parity + j, rows(t["gmlp_w_out"], l * 2 + j)) for j in range(2)])
        for n in range(2):
            sp.wait_ge(sem["yo_done"], n + 1)
            sp.dma_start(t["out"][n * P:(n + 1) * P, :], yo[:, n, :]).then_inc(sem["out_done"], 16)
        sp.wait_ge(sem["out_done"], 32)

    @block.gpsimd
    def _(pool):
        pool.wait_ge(sem["act"], 1)

        def load(w, col, kk, g):
            src = w.rearrange("(k p) c -> p k c", p=P)[:, 2 * kk:2 * kk + 2]
            src = src[:, :, col] if isinstance(col, slice) else src[:, :, bass.ds(col, D)]
            pool.dma_start(m_raw[:, kk % 2, :, :], src).then_inc(m_full[kk % 2], 16)

        def job(w, col, vec, j, slot):
            seq = j * (2 * KC - 2)
            pool.wait_ge(sem["acc_done"], j + 1)
            pool.sem_inc(sem["pool_held"], 1)
            for kk in range(2):
                load(w, col, kk, 0)
            pool.wait_ge(sem["mod_red"], j + 1)
            n = 0
            for k in range(KC):
                if k % 2 == 0:
                    pool.wait_ge(m_full[(k // 2) % 2], (j * 2 + (k // 4) + 1) * 16)
                    pool.sem_inc(sem["pool_held"], 1)
                src = m_raw[:, (k // 2) % 2, k % 2, :]
                dst = m_acc[:, slot, :] if k == 0 else src
                nc.gpsimd.tensor_scalar(dst, src, silu_c[:, vec * KC + k:vec * KC + k + 1], 0.0,
                                        ALU.mult, ALU.add).then_inc(sem["pool_seq"], 1)
                n += 1
                if k:
                    pool.wait_ge(sem["pool_seq"], seq + n)
                    add = nc.gpsimd.tensor_tensor(m_acc[:, slot, :], m_acc[:, slot, :], src, ALU.add)
                    add.then_inc(sem["pool_seq"] if k < KC - 1 else sem["acc_done"], 1)
                    n += 1
                if k in (1, 3):
                    pool.wait_ge(sem["pool_seq"], seq + n)
                    pool.sem_inc(sem["pool_held"], 1)
                    load(w, col, k // 2 + 2, 0)

        def modules(layer, vecs, m0, n, j0):
            w = t["mod_w"][layer]

            def two(i, j):
                if len(vecs) == 2:
                    for v in vecs:
                        job(w, (i + m0) * D, v, j + v, (j0 + v) % 2)
                else:
                    for r in range(2):
                        job(w, (i * 2 + (m0 + r)) * D, vecs[0], j + r, (j0 + r) % 2)

            rounds = n if len(vecs) == 2 else n // 2
            with pool.Fori(0, rounds) as i:
                two(i, i * 2 + j0)
            if rounds * 2 // len(vecs) < n:
                c = (m0 + n - 1) * D
                job(w, slice(c, c + D), vecs[0], j0 + n - 1, (j0 + n - 1) % 2)

        modules(0, (0, 1), 2, 3, 0)
        modules(0, (0,), 5, 4, 6)

        s = STEPS[AB]
        pool.wait_ge(sem["lo_done"], 2 * (s.pA + 1))

        def split(pair):
            for j in range(2):
                slot = 2 * ((s.pA + pair) % 2) + j
                pool.wait_ge(sem["hi_done"], 2 * (s.pA + pair) + j + 1)
                nc.gpsimd.tensor_tensor(w_lo[:, slot, :], w_raw[:, slot, :], w_hi[:, slot, :].bitcast(F32),
                                        ALU.subtract).then_inc(sem["lo_done"], 1)

        for pair in (1, 2, 3):
            split(pair)
        for h in range(HEADS):
            for L in range(1, LEVELS + 1):
                if L == 1:
                    pool.wait_ge(sem["q_init"], h + 1)
                else:
                    pool.wait_ge(sem["f_merged"], 7 * h + L - 1)
                pool.wait_ge(sem["gathered"], 16 * h + 2 * L)
                q = picked_q(h % 2, 1 << (L - 1))
                nc.gpsimd.tensor_tensor(q, q, other_q(1 << (L - 1)), ALU.mult).then_inc(
                    sem["q_upd"] if L < LEVELS else sem["q_final"], 1)
            split(4 + 2 * h)
            split(5 + 2 * h)
        split(16)
        modules(1, (0,), 0, 9, 10)

    @block.scalar
    def _(act):
        def split(n, slot):
            act.wait_ge(raw_full[slot], raw_count(n, slot))
            act.wait_ge(sem["tile_used"], n + 1)
            nc.scalar.activation(w_hi[:, slot, :], w_raw[:, slot, :], ACT.Copy).then_inc(sem["hi_done"], 1)

        def split_next(l, p0, parity):
            for j in range(2):
                split((l + (p0 + 1)) * 2 + j, 2 * (1 - parity) + j)

        def publish(u, dst, bias=None):
            act.wait_ge(sem["t_done"], u + 1)
            if bias is None:
                nc.scalar.activation(dst, tbuf[:, u % 3, :], ACT.Copy).then_inc(sem["xhi_done"], 1)
            else:
                nc.scalar.activation(dst, tbuf[:, u % 3, :], ACT.Identity, bias=bias).then_inc(sem["xhi_done"], 1)

        def norm(nrm, ev, T, shifts, u0):
            for d in range(KC):
                act.wait_ge(sem["x_upd"], 8 * ev + d + 1)
                i = 8 * nrm + d
                if i >= 2:
                    act.wait_ge(sem["sq_used"], i - 1)
                nc.scalar.activation(sq[:, d % 2, tok(T)], xT[:, d, tok(T)], ACT.Square).then_inc(sem["sq_done"], 1)
            act.wait_ge(sem["sq_used"], 8 * nrm + 8)
            nc.scalar.activation(rms[:, tok(T)], ps[:, ssq_bank(T), tok(T)], ACT.Sqrt, bias=eps[:, 0:1],
                                 scale=1.0 / D).then_inc(sem["rms_done"], 1)
            if shifts is None:
                return
            for u, (k, c) in enumerate(norm_units(T)):
                publish(u0 + u, xn_hi[:, k, c * LAT:(c + 1) * LAT], shifts[c][:, k:k + 1])

        act.wait_ge(sem["dve"], DVE_PARAMS)
        nc.scalar.activation(silu_c[:, :], par[:, C_C:C_C + 2 * KC], ACT.Silu).then_inc(sem["act"], 1)
        act.wait_ge(sem["dve"], DVE_LB)
        nc.scalar.activation(lb_t[:, 0:2, :], lb_t[:, 0:2, :], ACT.Exp).then_inc(sem["act"], 1)
        split(0, 0)
        split(1, 1)
        for si, s in enumerate(STEPS):
            if s.kind == "ffn":
                if not (si == 1):
                    norm(NRM[si], EV_BEFORE[si], s.T, shift_of(mod_cols, s.layer, 6 * s.j, s.T),
                         U0[si])

                def up(l, parity):
                    split_next(l, s.pA, parity)
                    act.wait_ge(sem["tile_used"], (l + s.pA) * 2 + 1 + SLOTS)
                    act.wait_ge(sem["gated"], l + (s.q0 + 1))
                    nc.scalar.activation(act_s[:, qpar(s, parity), tok(s.T)], ps[:, 2 * parity, tok(s.T)],
                                         ACT.Silu).then_inc(sem["silu_done"], 1)
                    act.wait_ge(sem["gated"], l + (s.q0 + 3))
                    nc.scalar.activation(h_at(h_hi, s.T, l), hm[:, qpar(s, parity), tok(s.T)],
                                         ACT.Copy).then_inc(sem["hhi_done"], 1)

                in_pairs(act, s.pA, s.nf, up)
                n_down = s.nf // 2
                if s.pEnd == N_PAIRS:
                    n_down -= 1
                in_pairs(act, s.pB, n_down, lambda l, parity: split_next(l, s.pB, parity))
            elif s.kind == "ab":
                norm(NRM[si], EV_BEFORE[si], BOTH, shift_of(mod_cols, 0, 3, BOTH), U0[si])

                def split_pair(pair):
                    for j in range(2):
                        split(2 * (s.pA + pair) + j, 2 * ((s.pA + pair) % 2) + j)

                def bank(pair, j):
                    return ps[:, 2 * ((s.pA + pair) % 2) + j, :]

                def projected(pair, j):
                    act.wait_ge(sem["tile_used"], 2 * (s.pA + pair) + SLOTS + 1 + j)

                def gathers(h, levels):
                    for L in levels:
                        B = 1 << (L - 1)
                        if L == 1:
                            act.wait_ge(sem["f_done"], 2 * h + 2)
                            if h >= 1:
                                act.wait_ge(sem["lvl_done"], 5 * h)
                        else:
                            act.wait_ge(sem["k_upd"], 7 * h + L - 1)
                        nc.scalar.activation(as3(Kc[:, L, :], B), picked_k(h % 2, B, True), ACT.Copy).then_inc(sem["gathered"], 1)
                        if L == 1:
                            act.wait_ge(sem["q_init"], h + 1)
                        else:
                            act.wait_ge(sem["q_upd"], 7 * h + L - 1)
                        nc.scalar.activation(as3(Qc[:, L, :], B), picked_q(h % 2, B), ACT.Copy).then_inc(sem["gathered"], 1)

                def forget_sigmoid(h, j):
                    if j == 0 and h >= 1:
                        act.wait_ge(sem["f_done"], 2 * h)
                    projected(1 + 2 * h, j)
                    nc.scalar.activation(act_s[:, j, :], bank(1 + 2 * h, j), ACT.Sigmoid).then_inc(sem["sig_done"], 1)

                def gate_sigmoid(g, j):
                    projected(13 + g, j)
                    if g == 0:
                        act.wait_ge(sem[("q_init", "vt_done")[j]], HEADS)
                    else:
                        act.wait_ge(sem["g_done"], 2 * g - 1 + j)
                    nc.scalar.activation(hm[:, j, 0:LAT], bank(13 + g, j)[:, 0:LAT], ACT.Sigmoid).then_inc(sem["g_sig"], 1)

                def outputs(h):
                    act.wait_ge(sem["o_done"], h + 1)
                    nc.scalar.activation(osq, ps[:, 6, 0:LAT], ACT.Square)
                    nc.scalar.activation(Os[:, h, :], ps[:, 6, 0:LAT], ACT.Copy).then_inc(sem["o_copied"], 1)

                def output_rms(h):
                    act.wait_ge(sem["oss_done"], h + 1)
                    if h >= 1:
                        act.wait_ge(sem["o_scaled"], h)
                    nc.scalar.activation(orms, ps[:, 7, 0:LAT], ACT.Sqrt, bias=eps[:, 0:1], scale=1.0 / DH).then_inc(sem["orms_done"], 1)

                split_pair(1)
                projected(0, 1)
                act.wait_ge(sem["pool_w"], 1)
                nc.scalar.activation(rows_of(xp, 1), bank(0, 1)[:, 0:LAT].rearrange("p (r c) -> p r c", r=ROWS), ACT.Copy).then_inc(sem["pool_in"], 1)
                split_pair(2)
                forget_sigmoid(0, 0)
                forget_sigmoid(0, 1)
                split_pair(3)
                for h in range(HEADS):
                    qv = 2 + 2 * h
                    projected(qv, 0)
                    if h >= 1:
                        act.wait_ge(sem["q_init"], h)
                    nc.scalar.activation(hm[:, 0, 0:LAT], bank(qv, 0)[:, 0:LAT], ACT.Sigmoid).then_inc(sem["g_sig"], 1)
                    gathers(h, (1, 2, 3))
                    projected(qv, 1)
                    nc.scalar.activation(hm[:, 1, :], bank(qv, 1), ACT.Copy).then_inc(sem["v_raw"], 1)
                    gathers(h, (4, 5))
                    if h >= 1:
                        outputs(h - 1)
                    gathers(h, (6,))
                    act.wait_ge(sem["vt_done"], h + 1)
                    nc.scalar.activation(Vd[:, h % 2, :, :], bank(qv, 1).rearrange("p (a b) -> p a b", a=4), ACT.Copy).then_inc(sem["v_done"], 1)
                    gathers(h, (7, 8))
                    split_pair(qv + 2)
                    for j in range(2):
                        if h < HEADS - 1:
                            forget_sigmoid(h + 1, j)
                        else:
                            gate_sigmoid(0, j)
                        if j == 0 and h >= 1:
                            output_rms(h - 1)
                    split_pair(qv + 3)
                    act.wait_ge(sem["kt_done"], h + 1)
                    nc.scalar.activation(kT[:, :, :], ps[:, 7, :].rearrange("p (a b) -> p a b", a=4), ACT.Copy).then_inc(sem["kt_copied"], 1)
                    act.wait_ge(sem["s_done"], h + 1)
                    nc.scalar.activation(Sd[:, :, :], ps[:, 7, 0:2 * DH].rearrange("p (a b) -> p a b", a=2), ACT.Copy).then_inc(sem["s_copied"], 1)
                gate_sigmoid(1, 0)
                gate_sigmoid(1, 1)
                split_pair(16)
                outputs(HEADS - 1)
                gate_sigmoid(2, 0)
                gate_sigmoid(2, 1)
                output_rms(HEADS - 1)
                for c in range(KC):
                    publish(U0[si] + 16 + c, xn_hi[:, c, 0:LAT])
                in_pairs(act, s.pB, 4, lambda l, parity: split_next(l, s.pB, parity))
            else:
                norm(NRM[si], EV_BEFORE[si], LAT, shift_of(mod_cols, 1, 3, LAT), U0[si])
                act.wait_ge(sem["ws_t"], 1)
                nc.scalar.activation(wsT[:, :, :], ps[:, 6:8, :].rearrange("p a (g q) -> p (a g) q", q=P), ACT.Copy).then_inc(sem["wsT_done"], 1)

                def value_in(l, parity, dst):
                    split_next(l, s.pA if dst is Ug else s.pA + 4, parity)
                    for j in range(2):
                        n = (l + (s.pA if dst is Ug else s.pA + 4)) * 2 + (j + 1 + SLOTS)
                        act.wait_ge(sem["tile_used"], n)
                        src = ps[:, 2 * parity + j, 0:LAT]
                        g = l * 2 + j
                        if dst is Ug:
                            out = dst[:, g, :] if isinstance(g, int) else dst[:, bass.ds(g, 1), :]
                            src = src if isinstance(g, int) else src.rearrange("p (a b) -> p a b", a=1)
                            nc.scalar.activation(out, src, ACT.Gelu_apprx_tanh).then_inc(sem["u_done"], 1)
                        else:
                            out = dst[:, :, g * P:(g + 1) * P] if isinstance(g, int) else dst[:, :, bass.ds(g * P, P)]
                            nc.scalar.activation(out, src.rearrange("p (a b) -> p a b", a=2), ACT.Gelu_apprx_tanh).then_inc(sem["u_done"], 1)

                in_pairs(act, s.pA, 4, lambda l, parity: value_in(l, parity, Ug))
                in_pairs(act, s.pA + 4, 4, lambda l, parity: value_in(l, parity, Vt))
                for n in range(2):
                    act.wait_ge(sem["ln_d"], 3 * n + 2)
                    nc.scalar.activation(ps[:, 4:6, :].rearrange("p a b -> p (a b)"), Vt[:, n, :], ACT.Square,
                                         accum_out=stat[:, 2:3]).then_inc(sem["ln_a"], 1)
                    act.wait_ge(sem["ln_a"], 2 * n + 1)
                    nc.scalar.activation(stat[:, 3:4], stat[:, 2:3], ACT.Sqrt, bias=eps[:, 0:1], scale=1.0 / D).then_inc(sem["ln_a"], 1)
                for g in range(GROUPS):
                    publish(U0[si] + 8 + g, xn_hi[:, g, 0:LAT])
                in_pairs(act, s.pB, 4, lambda l, parity: split_next(l, s.pB, parity))
        norm(NRM[7], 7, LAT, None, 0)

    @block.vector
    def _(dve):
        chain = [0]

        def link(ins):
            chain[0] += 1
            ins.then_inc(sem["dve"], 1)
            dve.wait_ge(sem["dve"], chain[0])

        def split(n, slot):
            dve.wait_ge(sem["hi_done"], n + 1)
            nc.vector.tensor_tensor(w_lo[:, slot, :], w_raw[:, slot, :], w_hi[:, slot, :].bitcast(F32),
                                    ALU.subtract).then_inc(sem["lo_done"], 1)

        def split_next(l, p0, parity):
            for j in range(2):
                split((l + (p0 + 1)) * 2 + j, 2 * (1 - parity) + j)

        def slot_read(u):
            if u >= 3:
                dve.wait_ge(sem["xn_done"], u - 2)

        def publish(u, dst_hi, dst_lo, bias=None):
            dve.wait_ge(sem["xhi_done"], u + 1)
            hi = dst_hi.bitcast(F32)
            if bias is None:
                ins = nc.vector.tensor_tensor(dst_lo, tbuf[:, u % 3, :], hi, ALU.subtract)
            else:
                ins = nc.vector.scalar_tensor_tensor(out=dst_lo, in0=tbuf[:, u % 3, :], scalar=bias, in1=hi,
                                                     op0=ALU.add, op1=ALU.subtract)
            ins.then_inc(sem["xn_done"], 1)

        def norm(nrm, T, scales, shifts, u0):
            dve.wait_ge(sem["rms_done"], nrm + 1)
            nc.vector.reciprocal(rstd[:, tok(T)], rms[:, tok(T)]).then_inc(sem["rstd_done"], 1)
            dve.wait_ge(sem["rstd_done"], nrm + 1)
            if scales is None:
                for k in range(KC):
                    nc.vector.scalar_tensor_tensor(out=yT[:, k, :], in0=xT[:, k, 0:LAT], scalar=par[:, C_FINAL + k:C_FINAL + k + 1],
                                                   in1=rstd[:, 0:LAT], op0=ALU.mult, op1=ALU.mult).then_inc(sem["y_done"], 1)
                return
            units = norm_units(T)

            def scaled(u):
                k, c = units[u]
                slot_read(u0 + u)
                nc.vector.scalar_tensor_tensor(out=tbuf[:, (u0 + u) % 3, :], in0=xT[:, k, c * LAT:(c + 1) * LAT],
                                               scalar=scales[c][:, k:k + 1], in1=rstd[:, c * LAT:(c + 1) * LAT],
                                               op0=ALU.mult, op1=ALU.mult).then_inc(sem["t_done"], 1)

            scaled(0)
            for u, (k, c) in enumerate(units):
                if u + 1 < len(units):
                    scaled(u + 1)
                cc = slice(c * LAT, (c + 1) * LAT)
                publish(u0 + u, xn_hi[:, k, cc], xn_lo[:, k, cc], shifts[c][:, k:k + 1])

        def finish_mod(row, m, src, n=KC):
            layer = 1 if row == 2 else 0
            dst = mods[:, row, m * KC:(m + 1) * KC]
            ins = nc.vector.tensor_tensor(dst, src, mod_b[:, layer, m * KC:(m + 1) * KC], ALU.add)
            if m % 3 == 1:
                link(ins)
                g = C_NORM + (layer * 3 + m // 3) * KC
                ins = nc.vector.scalar_tensor_tensor(out=dst, in0=dst, scalar=1.0, in1=par[:, g:g + KC],
                                                     op0=ALU.add, op1=ALU.mult)
            elif m in (2, 8):
                link(ins)
                ins = nc.vector.tensor_scalar(dst, dst, 0.5, None, ALU.mult)
            return ins

        def take_jobs(jobs):
            if jobs:
                dve.wait_ge(sem["mod_red"], jobs[-1] + 3)
            for j in jobs:
                layer, vec, m = JOBS[j]
                finish_mod(2 if layer else vec, m, ps[:, 7, (j % 2) * KC:(j % 2 + 1) * KC]).then_inc(sem["mod_fin"], 1)
                dve.wait_ge(sem["mod_fin"], j + 2)

        def evict(ev, T, tiles, gates):
            dve.wait_ge(sem["tile_used"], tiles + SLOTS)
            for d in range(KC):
                y = y_at(T, d)
                for c in range(T // LAT):
                    cc = slice(c * LAT, (c + 1) * LAT)
                    ins = nc.vector.scalar_tensor_tensor(out=xT[:, d, cc], in0=y if T == LAT else y[:, cc],
                                                         scalar=gates[c][:, d:d + 1], in1=xT[:, d, cc],
                                                         op0=ALU.mult, op1=ALU.add)
                ins.then_inc(sem["x_upd"], 1)

        nc.vector.memset(ones[:, :], 1.0)
        link(nc.vector.memset(eps[:, :], EPS))
        for s_, n_ in ((sem["tile_used"], SLOTS), (sem["gated"], 2), (sem["mod_red"], 2), (sem["acc_done"], 1)):
            dve.sem_inc(s_, n_)
        dve.wait_ge(sem["consts"], 48)
        nc.vector.tensor_copy(masks[:, :, :], masks_in[:, :, :])
        dve.wait_ge(sem["pe_x"], 1)
        nc.vector.tensor_copy(par[:, :], ps[:, 0, 0:N_PAR])
        link(nc.vector.tensor_copy(mod_b[:, :, :], ps[:, 0, P:P + 2 * P].rearrange("p (a b) -> p a b", a=2)[:, :, 0:N_MOD * KC]))
        assert chain[0] == DVE_PARAMS
        L0, L1 = par[:, C_LB:C_LB + 12], par[:, C_LB + 12:C_LB + 24]
        link(nc.vector.tensor_tensor(lb_t[:, 2, :], L0, L1, ALU.max))
        nc.vector.tensor_tensor(lb_t[:, 0, :], L0, lb_t[:, 2, :], ALU.subtract)
        link(nc.vector.tensor_tensor(lb_t[:, 1, :], L1, lb_t[:, 2, :], ALU.subtract))
        assert chain[0] == DVE_LB
        for k in range(KC):
            dve.wait_ge(sem["pe_x"], 2 + k)
            nc.vector.tensor_copy(xT[:, k, :], ps[:, X_BANKS[k % 4], :]).then_inc(sem["x_upd"], 1)
        dve.wait_ge(sem["act"], 2)
        link(nc.vector.tensor_tensor(lb_t[:, 2, :], lb_t[:, 0, :], lb_t[:, 1, :], ALU.add))
        link(nc.vector.reciprocal(lb_t[:, 3, :], lb_t[:, 2, :]))
        nc.vector.tensor_tensor(one_lb[:, :], lb_t[:, 1, :], lb_t[:, 3, :], ALU.mult)
        link(nc.vector.tensor_tensor(lb[:, :], lb_t[:, 0, :], lb_t[:, 3, :], ALU.mult))
        split(0, 0)
        split(1, 1)
        dve.wait_ge(sem["first_red"], 4)
        sums = ps[:, 5, 0:4 * KC].rearrange("p (c two) -> p two c", two=2)
        for m in range(2):
            for v in range(2):
                link(finish_mod(v, m, sums[:, v, m * KC:(m + 1) * KC]))
        nc.vector.tensor_copy(stat[:, 7:8], eps[:, 0:1]).then_inc(sem["mod_fin"], 1)

        for si, s in enumerate(STEPS):
            if s.kind == "ffn":
                m0 = 0 if s.j == 0 else 6
                if si != 1:
                    norm(NRM[si], s.T, shift_of(mod_cols, s.layer, m0 + 1, s.T), shift_of(mod_cols, s.layer, m0, s.T), U0[si])

                def up(l, parity):
                    split_next(l, s.pA, parity)
                    dve.wait_ge(sem["silu_done"], l + (s.q0 + 1))
                    dve.wait_ge(sem["tile_used"], (l + s.pA) * 2 + 2 + SLOTS)
                    dve.wait_ge(sem["lo_done"], (l + s.pA) * 2 + 2)
                    qp = qpar(s, parity)
                    nc.vector.tensor_tensor(hm[:, qp, tok(s.T)], act_s[:, qp, tok(s.T)], ps[:, 2 * parity + 1, tok(s.T)],
                                            ALU.mult).then_inc(sem["gated"], 1)
                    dve.wait_ge(sem["hhi_done"], l + (s.q0 + 1))
                    nc.vector.tensor_tensor(h_at(h_lo, s.T, l), hm[:, qp, tok(s.T)], h_at(h_hi, s.T, l).bitcast(F32),
                                            ALU.subtract).then_inc(sem["hlo_done"], 1)

                with_jobs(dve, si, 0, up, take_jobs)
                n_down = s.nf // 2 - (s.pEnd == N_PAIRS)
                in_pairs(dve, s.pB, n_down, lambda l, parity: split_next(l, s.pB, parity))
                evict(EV[si], s.T, 2 * s.pEnd, shift_of(mod_cols, s.layer, m0 + 2, s.T))
            elif s.kind == "ab":
                norm(NRM[si], BOTH, shift_of(mod_cols, 0, 4, BOTH), shift_of(mod_cols, 0, 3, BOTH), U0[si])
                take_jobs(JOBS_AT_AB)
                nc.vector.memset(xp[:, :, :], 0.0)
                nc.vector.memset(pw[:, :, :], 0.0).then_inc(sem["pool_w"], 1)

                def bank(pair, j):
                    return ps[:, 2 * ((s.pA + pair) % 2) + j, :]

                def queries(h):
                    hp = h % 2
                    dve.wait_ge(sem["g_sig"], h + 1)
                    if h >= 1:
                        dve.wait_ge(sem["lvl_done"], 5 * h)
                    if h >= 2:
                        dve.wait_ge(sem["o_done"], h - 1)
                    nc.vector.scalar_tensor_tensor(out=Qc[:, 0, :], in0=bank(2 + 2 * h, 0)[:, 0:LAT], scalar=float(DH) ** -0.5,
                                                   in1=hm[:, 0, 0:LAT], op0=ALU.mult, op1=ALU.mult).then_inc(sem["q_read"], 1)
                    dve.wait_ge(sem["f_done"], 2 * h + 2)
                    nc.vector.tensor_tensor(Kc[:, 0, :], Kd[:, hp, 0, 0:LAT], Kd[:, hp, 1, 0:LAT], ALU.add).then_inc(sem["kq0_done"], 1)
                    dve.wait_ge(sem["q_read"], h + 1)
                    nc.vector.tensor_tensor(Qd[:, hp, 0, :], Qc[:, 0, :], Fg[:, 1, 0:LAT], ALU.mult)
                    nc.vector.tensor_tensor(Qd[:, hp, 1, :], Qc[:, 0, :], Fg[:, 0, 0:LAT], ALU.mult).then_inc(sem["q_init"], 1)

                def updates(h):
                    hp = h % 2
                    if h >= 1:
                        dve.wait_ge(sem["q_final"], h)
                    for L in range(1, LEVELS):
                        B = 1 << (L - 1)
                        n = BOTH // B
                        buf, width, at = blocks(B)
                        left, right = (ap3(buf, width, at + o, (n, 2), (2, n // 2)) for o in (0, 1))
                        nc.vector.tensor_tensor(Fb[:, block_at(2 * B):block_at(2 * B) + n].rearrange("p (a b) -> p a b", a=2),
                                                left, right, ALU.mult).then_inc(sem["f_merged"], 1)
                        dve.wait_ge(sem["gathered"], 16 * h + 2 * L - 1)
                        if L == 1:
                            dve.wait_ge(sem["kq0_done"], h + 1)
                        k = picked_k(hp, B, False)
                        nc.vector.tensor_tensor(k, k, other_k(B), ALU.mult).then_inc(sem["k_upd"], 1)
                        dve.wait_ge(sem["f_merged"], 7 * h + L)
                    dve.wait_ge(sem["gathered"], 16 * h + 15)
                    dve.wait_ge(sem["k_upd"], 7 * h + 7)
                    k = picked_k(hp, P, False, True)
                    nc.vector.tensor_tensor(k, k, other_k(P, True), ALU.mult).then_inc(sem["k_final"], 1)

                def forget(h, j):
                    hp, c = h % 2, j * HEADS + h
                    dve.wait_ge(sem["sig_done"], 2 * h + j + 1)
                    if h >= 1:
                        dve.wait_ge(sem["q_upd"], 7 * h)
                    link(nc.vector.tensor_scalar(Fg[:, j, :], act_s[:, j, :], one_lb[:, c:c + 1], lb[:, c:c + 1],
                                                 ALU.mult, ALU.add))
                    if j == 0 and h >= 2:
                        dve.wait_ge(sem["kt_done"], h - 1)
                    nc.vector.tensor_scalar(Kd[:, hp, j, :], Fg[:, j, :], -1.0, 1.0, ALU.mult, ALU.add).then_inc(sem["f_done"], 1)

                def gate(g, j):
                    dve.wait_ge(sem["g_sig"], HEADS + 2 * g + j + 1)
                    nc.vector.tensor_tensor(Gs[:, 2 * g + j, :], bank(13 + g, j)[:, 0:LAT], hm[:, j, 0:LAT], ALU.mult).then_inc(sem["g_done"], 1)

                def scores(h, groups):
                    for b in groups:
                        i = 5 * h + b
                        dve.wait_ge(sem["lvl_done"], i + 1)
                        if b == 0 and h >= 1:
                            dve.wait_ge(sem["o_done"], h)
                        if b == 4:
                            nc.vector.tensor_copy(Ax[:, :, :], ps[:, 4 + i % 2, 0:2 * P].rearrange("p (a b) -> p a b", a=2)).then_inc(sem["cp_done"], 1)
                            continue
                        for L in (2 * b, 2 * b + 1):
                            src = ps[:, 4 + i % 2, (L % 2) * 2 * P:(L % 2) * 2 * P + 2 * P].rearrange("p (a b) -> p a b", a=2)
                            if L == 0:
                                ins = nc.vector.tensor_copy(Am[:, :, :], src)
                            else:
                                mask = ap3(masks, LEVELS * P, L * P, (0, 2), (1, P))
                                ins = nc.vector.copy_predicated(Am[:, :, :], mask, src)
                            if L % 2 == 0:
                                link(ins)
                        ins.then_inc(sem["cp_done"], 1)
                        dve.wait_ge(sem["cp_done"], i + 1)

                def scaled_output(h):
                    dve.wait_ge(sem["orms_done"], h + 1)
                    link(nc.vector.reciprocal(orstd, orms))
                    dve.wait_ge(sem["o_copied"], h + 1)
                    nc.vector.scalar_tensor_tensor(out=Os[:, h, :], in0=Os[:, h, :], scalar=par[:, C_HG + h:C_HG + h + 1],
                                                   in1=orstd, op0=ALU.mult, op1=ALU.mult).then_inc(sem["o_scaled"], 1)

                dve.wait_ge(sem["tile_used"], 2 * s.pA + SLOTS + 1)
                dve.wait_ge(sem["pool_w"], 1)
                nc.vector.tensor_copy(rows_of(xp, 0), bank(0, 0)[:, 0:LAT].rearrange("p (r c) -> p r c", r=ROWS)).then_inc(sem["pool_in"], 1)
                dve.wait_ge(sem["pool_in"], 2)
                pool_windows(nc, dve, link, xp, xs, py, inv_cnt, sem)
                forget(0, 0)
                forget(0, 1)
                for h in range(HEADS):
                    queries(h)
                    updates(h)
                    if h < HEADS - 1:
                        forget(h + 1, 0)
                    else:
                        gate(0, 0)
                    scores(h, (0, 1))
                    if h >= 1:
                        scaled_output(h - 1)
                    if h < HEADS - 1:
                        forget(h + 1, 1)
                    else:
                        gate(0, 1)
                    scores(h, (2, 3, 4))
                gate(1, 0)
                gate(1, 1)
                gate(2, 0)
                gate(2, 1)
                scaled_output(HEADS - 1)
                dve.wait_ge(sem["tile_used"], 2 * s.pB + SLOTS)
                u0 = U0[si] + 16
                dve.wait_ge(sem["pm_done"], 1)
                dve.wait_ge(sem["g_done"], HEADS)
                dve.wait_ge(sem["o_scaled"], HEADS)

                def mixed(c):
                    slot_read(u0 + c)
                    if c < POOL_TILES:
                        ins = nc.vector.tensor_scalar(tbuf[:, (u0 + c) % 3, :], ps[:, 7, c * LAT:(c + 1) * LAT],
                                                      par[:, C_PS + c:C_PS + c + 1], None, ALU.mult)
                    else:
                        ins = nc.vector.tensor_tensor(tbuf[:, (u0 + c) % 3, :], Os[:, c - 2, :], Gs[:, c - 2, :], ALU.mult)
                    ins.then_inc(sem["t_done"], 1)

                mixed(0)
                for c in range(KC):
                    if c + 1 < KC:
                        mixed(c + 1)
                    publish(u0 + c, xn_hi[:, c, 0:LAT], xn_lo[:, c, 0:LAT])
                dve.wait_ge(sem["lo_done"], 2 * (s.pB + 1))
                in_pairs(dve, s.pB, 4, lambda l, parity: split_next(l, s.pB, parity))
                evict(EV[si], LAT, 2 * s.pEnd, [mod_cols(0, 0, 5)])
            else:
                norm(NRM[si], LAT, [mod_cols(1, 0, 4)], [mod_cols(1, 0, 3)], U0[si])
                in_pairs(dve, s.pA, 8, lambda l, parity: split_next(l, s.pA, parity))
                dve.wait_ge(sem["u_done"], 16)
                dve.wait_ge(sem["gm_in"], 64)
                for n in range(2):
                    link(nc.vector.tensor_reduce(stat[:, 0:1], Vt[:, n, :], AX.X, ALU.add))
                    nc.vector.tensor_scalar(stat[:, 1:2], stat[:, 0:1], -1.0 / D, None, ALU.mult).then_inc(sem["ln_d"], 1)
                    dve.wait_ge(sem["ln_d"], 3 * n + 1)
                    nc.vector.tensor_scalar(Vt[:, n, :], Vt[:, n, :], stat[:, 1:2], None, ALU.add).then_inc(sem["ln_d"], 1)
                    dve.wait_ge(sem["ln_a"], 2 * n + 2)
                    link(nc.vector.reciprocal(stat[:, 4:5], stat[:, 3:4]))
                    link(nc.vector.scalar_tensor_tensor(out=Vt[:, n, :], in0=Vt[:, n, :], scalar=stat[:, 4:5], in1=ln_g[:, :],
                                                        op0=ALU.mult, op1=ALU.mult))
                    nc.vector.tensor_tensor(Vt[:, n, :], Vt[:, n, :], ln_b[:, :], ALU.add).then_inc(sem["ln_d"], 1)
                u0 = U0[si] + 8

                def gated(g):
                    dve.wait_ge(sem["sv_done"], g + 1)
                    slot_read(u0 + g)
                    bias = ap3(bs, D, g * P, (0, 2), (1, P))
                    link(nc.vector.tensor_tensor(sv[:, g % 2, :].rearrange("p (a b) -> p a b", a=2),
                                                 ps[:, 4 + g % 2, 0:LAT].rearrange("p (a b) -> p a b", a=2), bias, ALU.add))
                    nc.vector.tensor_tensor(tbuf[:, (u0 + g) % 3, :], sv[:, g % 2, :], Ug[:, g, :], ALU.mult).then_inc(sem["t_done"], 1)

                dve.wait_ge(sem["tile_used"], 2 * s.pB + SLOTS)
                gated(0)
                for g in range(GROUPS):
                    if g + 1 < GROUPS:
                        gated(g + 1)
                    publish(u0 + g, xn_hi[:, g, 0:LAT], xn_lo[:, g, 0:LAT])
                in_pairs(dve, s.pB, 4, lambda l, parity: split_next(l, s.pB, parity))
                evict(EV[si], LAT, 2 * s.pEnd, [mod_cols(1, 0, 5)])
        norm(NRM[7], LAT, None, None, 0)
        for n in range(2):
            dve.wait_ge(sem["yt_done"], n + 1)
            nc.vector.tensor_copy(yo[:, n, :], ps[:, 1 + 2 * n:3 + 2 * n, :].rearrange("p a b -> p (a b)")).then_inc(sem["yo_done"], 1)

    @block.tensor
    def _(pe):
        def product(out, st_hi, st_lo, mv_hi, mv_lo, start, stop, shared=False):
            nc.tensor.matmul(out, st_lo, mv_hi, start=start, stop=False, skip_group_check=shared)
            nc.tensor.matmul(out, st_hi, mv_lo, start=False, stop=False, skip_group_check=shared)
            return nc.tensor.matmul(out, st_hi, mv_hi, start=False, stop=stop, skip_group_check=shared)

        def tile_ready(n):
            pe.wait_ge(sem["hi_done"], n + 1)
            pe.wait_ge(sem["lo_done"], n + 1)

        def project(n, slot, T, c0=0, xn0=None):
            tile_ready(n)
            for k in range(KC):
                if xn0 is not None:
                    pe.wait_ge(sem["xn_done"], xn0 + (k + 1) * (T // LAT))
                w = slice(k * P, (k + 1) * P)
                last = product(ps[:, slot, 0:T], w_hi[:, slot, w], w_lo[:, slot, w],
                               xn_hi[:, k, 0:T], xn_lo[:, k, 0:T], k == 0, k == KC - 1)
            last.then_inc(sem["tile_used"], 1)

        def project_tokens(n, slot, tiles):
            tile_ready(n)
            for i in range(tiles):
                x = slice(i * P, (i + 1) * P)
                for k in range(KC):
                    w = slice(k * P, (k + 1) * P)
                    last = product(ps[:, slot, x], xn_hi[:, k, x], xn_lo[:, k, x],
                                   w_hi[:, slot, w], w_lo[:, slot, w], k == 0, k == KC - 1)
            last.then_inc(sem["tile_used"], 1)

        def down(n, slot, T, hi, lo, start, stop):
            tile_ready(n)
            for d in range(KC):
                w = slice(d * P, (d + 1) * P)
                last = product(y_at(T, d), w_hi[:, slot, w], w_lo[:, slot, w], hi, lo,
                               start and (T == BOTH or d % 2 == 0), stop, shared=True)
            last.then_inc(sem["tile_used"], 1)

        def norm(nrm, T):
            for d in range(KC):
                pe.wait_ge(sem["sq_done"], 8 * nrm + d + 1)
                mm = nc.tensor.matmul(ps[:, ssq_bank(T), tok(T)], ones[:, :], sq[:, d % 2, tok(T)],
                                      start=(d == 0), stop=(d == KC - 1))
                mm.then_inc(sem["sq_used"], 1)

        def take_jobs(jobs):
            if jobs:
                pe.wait_ge(sem["mod_fin"], jobs[0] + 1)
            for j in jobs:
                pe.wait_ge(sem["acc_done"], j + 2)
                for c in range(KC):
                    mm = nc.tensor.matmul(ps[:, 7, (j % 2) * KC + c:(j % 2) * KC + c + 1], m_acc[:, j % 2, c * P:(c + 1) * P], ones[:, 0:1],
                                          start=True, stop=True)
                mm.then_inc(sem["mod_red"], 1)

        pe.wait_ge(sem["consts"], 48)
        pe.wait_ge(sem["params"], 32)
        pe.wait_ge(sem["dve"], 1)
        nc.tensor.transpose(ps[:, 0, 0:N_PAR], par_rows[0:N_PAR, :], ident[0:N_PAR, 0:N_PAR])
        R = N_MOD * KC
        for l in range(2):
            mm = nc.tensor.transpose(ps[:, 0, P + l * P:P + l * P + R], mb_rows[0:R, l, :], ident[0:R, 0:R])
        mm.then_inc(sem["pe_x"], 1)
        pe.wait_ge(sem["xin_full"], 32)
        for k in range(KC):
            if k >= 4:
                pe.wait_ge(sem["x_upd"], k - 3)
            for n in range(4):
                mm = nc.tensor.transpose(ps[:, X_BANKS[k % 4], n * P:(n + 1) * P], xin[:, n, k * P:(k + 1) * P], ident[:, :])
            mm.then_inc(sem["pe_x"], 1)
        pe.wait_ge(sem["act"], 1)
        for g in range(4):
            pe.wait_ge([sem["m_first_full0"], sem["m_first_full1"]][g % 2], 16 * (g // 2 + 1))
            for kk in range(4):
                k = 4 * (g % 2) + kk
                for c in range(KC):
                    col = 2 * ((g // 2) * KC + c)
                    mm = nc.tensor.matmul(ps[:, 5, col:col + 2], m_first[:, k, c * P:(c + 1) * P], silu_c[:, k:2 * KC:KC],
                                          start=(g == 0 and kk == 0 and c == 0), stop=(k == KC - 1), skip_group_check=True)
            mm.then_inc(sem["first_red"], 1)

        for si, s in enumerate(STEPS):
            if s.kind == "ffn":
                if si != 1:
                    norm(NRM[si], s.T)
                else:
                    pe.wait_ge(sem["x_upd"], 8 * EV[0] + 8)
                pe.wait_ge(sem["gated"], s.q0 + 2)
                par0 = s.pA % 2
                project(2 * s.pA, 2 * par0, s.T, xn0=U0[si] if si != 1 else None)
                project(2 * s.pA + 1, 2 * par0 + 1, s.T)

                def up(l, parity):
                    pe.wait_ge(sem["gated"], l + (s.q0 + 1))
                    for j in range(2):
                        project((l + s.pA) * 2 + j, 2 * parity + j, s.T)

                with_jobs(pe, si, 1, up, take_jobs)
                pe.wait_ge(sem["mod_fin"], JOBS_AT[si][-1][1][-1] + 2)
                if s.T == BOTH:
                    pe.wait_ge(sem["gated"], s.q0 + s.nf + 2)

                def add(l, parity, start=False, stop=False, skip=0):
                    for j in range(2):
                        f = (l + skip) * 2 + j
                        pe.wait_ge(sem["hlo_done"], f + (s.q0 + 1))
                        down((l + (s.pB + skip)) * 2 + j, 2 * parity + j, s.T, h_at(h_hi, s.T, f), h_at(h_lo, s.T, f),
                             start and j == 0, stop and j == 1)

                n = s.nf // 2
                add(0, s.pB % 2, start=True)
                in_pairs(pe, s.pB + 1, n - 2, lambda l, parity: add(l, parity, skip=1))
                add(n - 1, (s.pB + n - 1) % 2, stop=True)
            elif s.kind == "ab":
                norm(NRM[si], BOTH)
                pe.wait_ge(sem["x_upd"], 8 * EV[1] + 8)
                take_jobs(JOBS_AT_AB)
                pe.wait_ge(sem["mod_fin"], JOBS_AT_AB[-1] + 2)
                pe.wait_ge(sem["xn_done"], U0[si] + 16)

                def banks_free(pair):
                    if pair == 2:
                        pe.wait_ge(sem["pool_in"], 2)
                    elif pair == 15:
                        pe.wait_ge(sem["g_done"], 2)
                    elif pair % 2:
                        pe.wait_ge(sem["sig_done"], pair - 1)
                    elif pair:
                        pe.wait_ge(sem["q_read"], pair // 2 - 1)
                        pe.wait_ge(sem["v_done"], pair // 2 - 1)

                def project_one(pair, j, T):
                    project(2 * (s.pA + pair) + j, 2 * ((s.pA + pair) % 2) + j, T)

                def levels(h, groups):
                    for b in groups:
                        i = 5 * h + b
                        if i >= 2:
                            pe.wait_ge(sem["cp_done"], i - 1)
                        if b == 0:
                            pe.wait_ge(sem["kq0_done"], h + 1)
                        pe.wait_ge(sem["gathered"], 16 * h + min(4 * b + 2, 16))
                        if b < 4:
                            for L in (2 * b, 2 * b + 1):
                                for n in range(2):
                                    at = (L % 2) * 2 * P + n * P
                                    x = slice(n * P, (n + 1) * P)
                                    mm = nc.tensor.matmul(ps[:, 4 + i % 2, at:at + P], Kc[:, L, x], Qc[:, L, x], start=True, stop=True)
                        else:
                            for n in range(2):
                                mm = nc.tensor.matmul(ps[:, 4 + i % 2, n * P:(n + 1) * P], Kc[:, LEVELS, n * P:(n + 1) * P],
                                                      Qc[:, LEVELS, (1 - n) * P:(2 - n) * P], start=True, stop=True)
                        mm.then_inc(sem["lvl_done"], 1)

                def turned_keys(h):
                    pe.wait_ge(sem["k_final"], h + 1)
                    if h >= 1:
                        pe.wait_ge(sem["orms_done"], h)
                    for d in range(2):
                        for n in range(2):
                            mm = nc.tensor.transpose(ps[:, 7, (2 * d + n) * P:(2 * d + n + 1) * P],
                                                     Kd[:, h % 2, d, LAT + n * P:LAT + (n + 1) * P], ident[:, :])
                    mm.then_inc(sem["kt_done"], 1)

                def states(h):
                    pe.wait_ge(sem["kt_copied"], h + 1)
                    pe.wait_ge(sem["v_done"], h + 1)
                    for d in range(2):
                        for n in range(2):
                            mm = nc.tensor.matmul(ps[:, 7, d * DH:(d + 1) * DH], kT[:, 2 * d + n, :], Vd[:, h % 2, 2 + n, :],
                                                  start=(n == 0), stop=(n == 1))
                    mm.then_inc(sem["s_done"], 1)

                def outputs(h):
                    hp = h % 2
                    pe.wait_ge(sem["s_copied"], h + 1)
                    pe.wait_ge(sem["q_final"], h + 1)
                    pe.wait_ge(sem["cp_done"], 5 * h + 5)
                    if h >= 1:
                        pe.wait_ge(sem["o_copied"], h)
                    o = ps[:, 6, :]
                    nc.tensor.matmul(o[:, 0:LAT], Sd[:, 0, :], Qd[:, hp, 1, :], start=True, stop=False, skip_group_check=True)
                    nc.tensor.matmul(o[:, 0:LAT], Sd[:, 1, :], Qd[:, hp, 0, :], start=False, stop=False, skip_group_check=True)
                    for n in range(2):
                        x, y = slice(n * P, (n + 1) * P), slice((1 - n) * P, (2 - n) * P)
                        nc.tensor.matmul(o[:, x], Vd[:, hp, n, :], Am[:, n, :], start=False, stop=False, skip_group_check=True)
                        mm = nc.tensor.matmul(o[:, y], Vd[:, hp, n, :], Ax[:, n, :], start=False, stop=(n == 1), skip_group_check=True)
                    mm.then_inc(sem["o_done"], 1)

                def output_squares(h):
                    pe.wait_ge(sem["o_copied"], h + 1)
                    nc.tensor.matmul(ps[:, 7, 0:LAT], ones[:, :], osq, start=True, stop=True).then_inc(sem["oss_done"], 1)

                for pair, T in ((0, LAT), (1, BOTH)):
                    project_one(pair, 0, T)
                    project_one(pair, 1, T)
                for h in range(HEADS):
                    qv = 2 + 2 * h
                    banks_free(qv)
                    project_one(qv, 0, LAT)
                    project_one(qv, 1, BOTH)
                    if h >= 1:
                        outputs(h - 1)
                    pe.wait_ge(sem["v_raw"], h + 1)
                    for n in range(4):
                        mm = nc.tensor.transpose(ps[:, 2 * ((s.pA + qv) % 2) + 1, n * P:(n + 1) * P], hm[:, 1, n * P:(n + 1) * P], ident[:, :])
                    mm.then_inc(sem["vt_done"], 1)
                    T = BOTH if h < HEADS - 1 else LAT
                    banks_free(qv + 1)
                    project_one(qv + 1, 0, T)
                    levels(h, (0, 1))
                    if h >= 1:
                        output_squares(h - 1)
                    project_one(qv + 1, 1, T)
                    levels(h, (2, 3))
                    turned_keys(h)
                    levels(h, (4,))
                    states(h)
                banks_free(14)
                project_one(14, 0, LAT)
                project_one(14, 1, LAT)
                outputs(HEADS - 1)
                banks_free(15)
                project_one(15, 0, LAT)
                project_one(15, 1, LAT)
                output_squares(HEADS - 1)
                pe.wait_ge(sem["orms_done"], HEADS)
                pe.wait_ge(sem["py_done"], 1)
                pe.wait_ge(sem["pool_w"], 1 + 64)
                for c in range(POOL_TILES):
                    mm = nc.tensor.matmul(ps[:, 7, c * LAT:(c + 1) * LAT], pw[:, c, :], py[:, c, :], start=True, stop=True)
                mm.then_inc(sem["pm_done"], 1)
                pe.wait_ge(sem["xn_done"], U0[si] + 16 + KC)
                for c in range(KC):
                    down(2 * s.pB + c, (2 * s.pB + c) % SLOTS, LAT, xn_hi[:, c, 0:LAT], xn_lo[:, c, 0:LAT], c == 0, c == KC - 1)
            else:
                norm(NRM[si], LAT)
                pe.wait_ge(sem["gm_in"], 64)
                for g in range(GROUPS):
                    mm = nc.tensor.transpose(ps[:, 6 + g // 4, (g % 4) * P:(g % 4 + 1) * P], ws[:, g, :], ident[:, :])
                mm.then_inc(sem["ws_t"], 1)
                pe.wait_ge(sem["xn_done"], U0[si] + 8)
                for p in range(8):
                    par_ = (s.pA + p) % 2
                    for j in range(2):
                        if p >= 2:
                            pe.wait_ge(sem["u_done"], 2 * (p - 2) + j + 1)
                        if p < 4:
                            project(2 * (s.pA + p) + j, 2 * par_ + j, LAT)
                        else:
                            project_tokens(2 * (s.pA + p) + j, 2 * par_ + j, 2)
                pe.wait_ge(sem["wsT_done"], 1)
                pe.wait_ge(sem["ln_d"], 6)
                for g in range(GROUPS):
                    if g >= 2:
                        pe.wait_ge(sem["t_done"], U0[si] + 8 + g - 1)
                    for n in range(2):
                        mm = nc.tensor.matmul(ps[:, 4 + g % 2, n * P:(n + 1) * P], Vt[:, n, g * P:(g + 1) * P], wsT[:, g, :],
                                              start=True, stop=True)
                    mm.then_inc(sem["sv_done"], 1)
                pe.wait_ge(sem["xn_done"], U0[si] + 16)
                for c in range(KC):
                    down(2 * s.pB + c, (2 * s.pB + c) % SLOTS, LAT, xn_hi[:, c, 0:LAT], xn_lo[:, c, 0:LAT], c == 0, c == KC - 1)
        norm(NRM[7], LAT)
        for k in range(KC):
            pe.wait_ge(sem["y_done"], k + 1)
            for n in range(2):
                mm = nc.tensor.transpose(ps[:, 1 + 2 * n + k // 4, (k % 4) * P:(k % 4 + 1) * P], yT[:, k, n * P:(n + 1) * P], ident[:, :])
                if k == KC - 1:
                    mm.then_inc(sem["yt_done"], 1)


EV = {0: 1, 1: 2, 2: 3, 3: 4, 4: 5, 5: 6, 6: 7}
EV_BEFORE = {0: 0, 2: 2, 3: 3, 4: 4, 5: 5, 6: 6}
NRM = {0: 0, 2: 1, 3: 2, 4: 3, 5: 4, 6: 5, 7: 6}
U0 = {0: 0, 1: 16, 2: 16, 3: 40, 4: 48, 5: 56, 6: 72}
X_BANKS = (1, 2, 3, 6)
DVE_PARAMS, DVE_LB = 2, 4
AB = 2


def norm_units(T):
    return [(k, c) for k in range(KC) for c in range(T // LAT)]


def shift_of(mod_cols, layer, m, T):
    return [mod_cols(layer, c, m) for c in range(T // LAT)]


def raw_count(n, slot):
    return (n - slot) * (16 // SLOTS) + 16


def qpar(s, parity):
    return parity


def rows_of(xp, c):
    return xp[:, c, :].rearrange("p (r w) -> p r w", r=ROWS)[:, :, PAD:PAD + GRID_W]


def pool_windows(nc, dve, link, xp, xs, py, inv_cnt, sem):
    for c in range(POOL_TILES):
        cur, width = xp[:, c, :], 1
        n = ROWS * RW
        windows = ((2, 4), (8, 16))[c]
        for i in range(4):
            nxt = xs[:, i % 2, 0:n - width]
            link(nc.vector.tensor_tensor(nxt, cur[:, 0:n - width], cur[:, width:n], ALU.add))
            n -= width
            width *= 2
            cur = xs[:, i % 2, 0:n]
            if width in windows:
                half = windows.index(width)
                q = slice(64 * half, 64 * half + 64)
                start = PAD - width // 2
                full = bass.AP(xs, (i % 2) * ROWS * RW + start + 64 * half * 2 * ROWS * RW,
                               [[2 * ROWS * RW, 64], [RW, ROWS], [1, GRID_W]])
                cnt = bass.AP(inv_cnt, c * GRID_W + 64 * half * POOL_TILES * GRID_W,
                              [[POOL_TILES * GRID_W, 64], [0, ROWS], [1, GRID_W]])
                out = py[q, c, :].rearrange("p (r w) -> p r w", r=ROWS)
                link(nc.vector.tensor_tensor(out, full, cnt, ALU.mult))
                last = nc.vector.tensor_tensor(out, out, rows_of(xp, c)[q], ALU.subtract)
                link(last)
                if width == windows[1]:
                    break
    nc.vector.tensor_copy(py[:, 0, 0:1], py[:, 0, 0:1]).then_inc(sem["py_done"], 1)


def constants():
    i, j = np.arange(P)[:, None], np.arange(P)[None, :]
    masks = np.zeros((P, LEVELS, P), np.float32)
    masks[:, 0] = i == j
    for L in range(1, LEVELS):
        B = 1 << (L - 1)
        masks[:, L] = (i // (2 * B) == j // (2 * B)) & (i // B != j // B)
    inv = np.zeros((P, POOL_TILES, GRID_W), np.float32)
    pos = np.arange(GRID_W)
    for g, w in enumerate((2, 4, 8, 16)):
        lo, hi = np.clip(pos - w // 2, 0, GRID_W), np.clip(pos - w // 2 + w, 0, GRID_W)
        inv[64 * (g % 2):64 * (g % 2) + 64, g // 2] = 1.0 / (hi - lo)
    return {"ident": np.eye(P, dtype=np.float32), "masks": masks, "inv_cnt": inv}


def kernel(x, c, ctx, c_ctx, mod_w, mod_b, norm_g, ffn_w1, ffn_w3, ffn_w2, ab_w_in, pool_w, pool_scale,
           hgrn_lb, hgrn_norm_g, ab_w_out, gmlp_w_in, gmlp_ln_g, gmlp_ln_b, gmlp_w_s, gmlp_b_s,
           gmlp_w_out, final_g):
    import concourse.bacc as bacc
    from concourse.bass_utils import run_bass_kernel_spmd

    def flat(a, *shape):
        return np.ascontiguousarray(np.asarray(a).reshape(shape))

    params = np.concatenate([np.asarray(a).reshape(-1, P) for a in
                             (norm_g, final_g, hgrn_lb, hgrn_norm_g, pool_scale, c, c_ctx)])
    arrays = dict(
        x=flat(x, LAT, D), ctx=flat(ctx, CTX, D), params=params, mod_w=flat(mod_w, 2, D, N_MOD * D),
        mod_b=flat(mod_b, 2, N_MOD * D), w1=flat(ffn_w1, 2, 2, D, FF), w3=flat(ffn_w3, 2, 2, D, FF),
        w2=flat(ffn_w2, 2, 2, FF, D), ab_w_in=flat(ab_w_in, D, -1), pool_w=flat(pool_w, 4, 64, 64),
        ab_w_out=flat(ab_w_out, D, D), gmlp_w_in=flat(gmlp_w_in, D, 2 * D), gmlp_ln_g=flat(gmlp_ln_g, D),
        gmlp_ln_b=flat(gmlp_ln_b, D), gmlp_w_s=flat(gmlp_w_s, GROUPS, P, P), gmlp_b_s=flat(gmlp_b_s, D),
        gmlp_w_out=flat(gmlp_w_out, D, D), **constants())
    nc = bacc.Bacc("TRN2", target_bir_lowering=False, num_devices=1)
    t = {}
    for name, a in arrays.items():
        t[name] = nc.dram_tensor(f"in_{name}", a.shape, mybir.dt.from_np(a.dtype), kind="ExternalInput").ap()
    t["out"] = nc.dram_tensor("out_y", (LAT, D), F32, kind="ExternalOutput").ap()
    build(nc, t)
    r = run_bass_kernel_spmd(nc, [{f"in_{k}": a for k, a in arrays.items()}], core_ids=[0])
    return r.results[0]["out_y"].reshape(1, LAT, D)
```

```python
from contextlib import ExitStack

import numpy as np

import concourse.bass as bass
from concourse import mybir

F32 = mybir.dt.float32
F32R = mybir.dt.float32r
U8 = mybir.dt.uint8
ALU = mybir.AluOpType
ACT = mybir.ActivationFunctionType
AX = mybir.AxisListType

P = 128
D = 1024
KC = D // P
LAT = 256
CTX = 256
BOTH = LAT + CTX
FF = 2816
NF = FF // P
NF_FIRST = 12
POOL_TILES = 2
HEADS = 6
DH = 128
GRID_W = 64
PAD = 8
ROWS = LAT // GRID_W
RW = GRID_W + 2 * PAD
N_MOD = 9
GROUPS = 8
EPS = 1e-6
LEVELS = 8
SLOTS = 4
FIRST_PAIRS = KC

C_NORM, C_LB, C_HG, C_PS, C_C, C_CC, N_PAR = 0, 48, 72, 78, 80, 88, 96


class Step:

    def __init__(self, kind, layer, pA, pB, pEnd):
        self.kind, self.layer, self.pA, self.pB, self.pEnd = kind, layer, pA, pB, pEnd


def plan():
    steps, p, q = [], FIRST_PAIRS, 0

    def ffn(layer, j, T, f0, nf):
        nonlocal p, q
        s = Step("ffn", layer, p, p + nf, p + nf + nf // 2)
        s.j, s.T, s.f0, s.nf, s.q0 = j, T, f0, nf, q
        p += nf + nf // 2
        q += nf
        steps.append(s)

    def mix(kind, layer, n_in, n_out):
        nonlocal p
        steps.append(Step(kind, layer, p, p + n_in, p + n_in + n_out))
        p += n_in + n_out

    ffn(0, 0, BOTH, 0, NF_FIRST)
    ffn(0, 0, BOTH, NF_FIRST, NF - NF_FIRST)
    mix("ab", 0, 16, 4)
    ffn(0, 1, LAT, 0, NF)
    ffn(1, 0, LAT, 0, NF)
    mix("gmlp", 1, 8, 4)
    ffn(1, 1, LAT, 0, NF)
    return steps, p


STEPS, N_PAIRS = plan()

JOBS = [(0, v, m) for m in (2, 3, 4) for v in (0, 1)] + [(0, 0, m) for m in range(5, 9)] \
    + [(1, 0, m) for m in range(9)]
JOBS_AT = {0: ((6, (0, 1)), (12, (2, 3))), 1: ((8, (6, 7)),), 3: ((8, (10, 11)),), 4: ((12, (14, 15)),), 6: ()}
JOBS_BEFORE = {0: (), 1: (4, 5), 2: (8, 9), 3: (), 4: (12, 13), 5: (16, 17), 6: (18,)}


def build(nc, t):
    stack = ExitStack()
    with stack:
        _build(nc, t, stack)


def _build(nc, t, stack):
    def sb(name, shape, dt=F32, within=stack):
        return within.enter_context(nc.sbuf_tensor(name, shape, dt))

    xT = sb("xT", [P, KC, BOTH])
    xn_hi = sb("xn_hi", [P, KC, BOTH], F32R)
    xn_lo = sb("xn_lo", [P, KC, BOTH], F32R)
    w_raw = sb("w_raw", [P, SLOTS, D])
    w_hi = sb("w_hi", [P, SLOTS, D], F32R)
    w_lo = sb("w_lo", [P, SLOTS, D], F32R)
    m_raw = sb("m_raw", [P, 2, 2, D])
    m_acc = sb("m_acc", [P, 2, D])
    rms = sb("rms", [P, BOTH])
    rstd = sb("rstd", [P, BOTH])
    sq = sb("sq", [P, 2, BOTH])
    tbuf = sb("tbuf", [P, 3, LAT])
    act_s = sb("act_s", [P, 2, BOTH])
    hm = sb("hm", [P, 2, BOTH])
    ident = sb("ident", [P, P])
    ones = sb("ones", [P, P])
    masks = sb("masks", [P, LEVELS, P], U8)
    inv_cnt = sb("inv_cnt", [P, POOL_TILES, GRID_W])
    par_rows = sb("par_rows", [P, P])
    mb_rows = sb("mb_rows", [P, 2, P])
    par = sb("par", [P, N_PAR])
    mod_b = sb("mod_b", [P, 2, N_MOD * KC])
    mods = sb("mods", [P, 3, N_MOD * KC])
    silu_c = sb("silu_c", [P, 2 * KC])
    silu_hi = sb("silu_hi", [P, 2 * KC], F32R)
    silu_lo = sb("silu_lo", [P, 2 * KC], F32R)
    lb_t = sb("lb_t", [P, 4, 2 * HEADS])
    lb = sb("lb", [P, 2 * HEADS])
    one_lb = sb("one_lb", [P, 2 * HEADS])
    eps = sb("eps", [P, 1])
    stat = sb("stat", [P, 8])

    part = ExitStack()
    xin = sb("xin", [P, 4, D], within=part)
    mod_row = sb("mod_row", [2, 2 * D], within=part)
    masks_in = sb("masks_in", [P, LEVELS, P], within=part)
    part.close()
    part = ExitStack()
    h_hi = sb("h_hi", [P, NF_FIRST * BOTH], F32R, within=part)
    h_lo = sb("h_lo", [P, NF_FIRST * BOTH], F32R, within=part)
    g_out = sb("g_out", [P, D], within=part)
    part.close()
    part = ExitStack()
    Fg = sb("Fg", [P, 2, BOTH], within=part)
    Fb = sb("Fb", [P, 2 * BOTH], within=part)
    Kd = sb("Kd", [P, 2, 2, BOTH], within=part)
    Qd = sb("Qd", [P, 2, 2, LAT], within=part)
    Vd = sb("Vd", [P, 2, 4, DH], within=part)
    Am = sb("Am", [P, 2, P], within=part)
    Ax = sb("Ax", [P, 2, P], within=part)
    kT = sb("kT", [P, 4, P], within=part)
    Sd = sb("Sd", [P, 2, DH], within=part)
    Gs = sb("Gs", [P, HEADS, LAT], within=part)
    Os = sb("Os", [P, HEADS, LAT], within=part)
    py = sb("py", [P, POOL_TILES, LAT], within=part)
    pw = sb("pw", [P, POOL_TILES, P], within=part)
    early = ExitStack()
    xp = sb("xp", [P, POOL_TILES, ROWS * RW], within=early)
    xs = sb("xs", [P, 2, ROWS * RW], within=early)
    early.close()
    early = ExitStack()
    Kc = sb("Kc", [P, LEVELS + 1, LAT], within=early)
    Qc = sb("Qc", [P, LEVELS + 1, LAT], within=early)
    early.close()
    mix_hi = sb("mix_hi", [P, KC, LAT], F32R, within=part)
    mix_lo = sb("mix_lo", [P, KC, LAT], F32R, within=part)
    part.close()
    osq, orms, orstd = rms[:, LAT:BOTH], rms[:, 0:LAT], rstd[:, 0:LAT]
    part = ExitStack()
    Ug = sb("Ug", [P, GROUPS, LAT], within=part)
    Vt = sb("Vt", [P, 2, D], within=part)
    ws = sb("ws", [P, GROUPS, P], within=part)
    wsT = sb("wsT", [P, GROUPS, P], within=part)
    ln_g = sb("ln_g", [P, D], within=part)
    ln_b = sb("ln_b", [P, D], within=part)
    bs = sb("bs", [P, D], within=part)
    sv = sb("sv", [P, 2, LAT], within=part)
    part.close()
    part = ExitStack()
    yo = sb("yo", [P, 2, D], within=part)
    part.close()

    ps = stack.enter_context(nc.psum_tensor("ps", [P, 8, 512], F32))

    sem = {name: stack.enter_context(nc.semaphore(name)) for name in (
        "consts tables params xin_full pool_w gm_in "
        "raw_full0 raw_full1 raw_full2 raw_full3 hi_done lo_done tile_used y_ready "
        "m_full0 m_full1 pool_seq pool_held acc_done mod_red mod_fin silu_split row_copied first_turned "
        "dve_chain act_setup turned_in x_upd sq_done sq_used sq_sum rms_done rstd_done t_done xhi_done xn_done "
        "silu_done gated hhi_done hlo_done "
        "pool_in q_read sig_done f_done v_raw vt_done v_done kq0_done q_init gathered k_upd f_merged q_upd k_final q_final lvl_done cp_done "
        "kt_done kt_copied s_done s_copied o_done o_copied oss_done orms_done o_scaled py_done pm_done pooled g_sig g_done "
        "v_gelu v_copied u_done ln_a ln_d ln_c ln_done ws_t wsT_done sv_done yt_done out_sq out_rms yo_done g_out_in out_done"
    ).split()}
    raw_full = [sem["raw_full0"], sem["raw_full1"], sem["raw_full2"], sem["raw_full3"]]
    m_full = [sem["m_full0"], sem["m_full1"]]

    def tok(T):
        return slice(0, T)

    def y_at(T, d):
        if T == BOTH:
            return ps[:, 4 + d if d < 4 else d - 4, :]
        return ps[:, 4 + d // 2, LAT * (d % 2):LAT * (d % 2) + LAT]

    def square_at(d, T):
        i = d % 6
        return (sq, act_s, hm)[i // 2][:, i % 2, tok(T)]

    def first_out(m):
        return ps[0:2, 1:3, :] if m == 0 else ps[0:2, 6:8, :]

    def out_rows(n):
        return ps[:, 2 * n:2 * n + 2, :].rearrange("p a b -> p (a b)")

    def ssq_bank(T):
        return 4 if T == BOTH else 0

    def mod_cols(layer, ctx, m):
        row = 2 if layer else ctx
        return mods[:, row, m * KC:(m + 1) * KC]

    def h_at(buf, T, f):
        return buf[:, f * T:(f + 1) * T] if isinstance(f, int) else buf[:, bass.ds(f * T, T)]

    def ap3(buf, width, offset, *dims):
        return bass.AP(buf, offset, [[width, P], *[list(d) for d in dims]])

    def picked_k(par_, B, lat_only, ctx_only=False):
        n, off = (LAT if lat_only or ctx_only else BOTH), par_ * 2 * BOTH + (LAT if ctx_only else 0)
        return ap3(Kd, 4 * BOTH, off, (2 * B, n // (2 * B)), (BOTH + B, 2), (1, B))

    def picked_q(par_, B):
        return ap3(Qd, 4 * LAT, par_ * 2 * LAT, (2 * B, LAT // (2 * B)), (LAT + B, 2), (1, B))

    def blocks(B):
        return (Fg, 2 * BOTH, 0) if B == 1 else (Fb, 2 * BOTH, block_at(B))

    def block_at(B):
        at, b = 0, 2
        while b < B:
            at += 2 * BOTH // b
            b *= 2
        return at

    def other_k(B, ctx_only=False):
        buf, width, at = blocks(B)
        n = BOTH // B
        pairs, skip = (CTX // (2 * B), LAT // B) if ctx_only else (n // 2, 0)
        return ap3(buf, width, at + skip + 1, (2, pairs), (n - 1, 2), (0, B))

    def other_q(B):
        buf, width, at = blocks(B)
        n = BOTH // B
        return ap3(buf, width, at + n + 1, (2, LAT // B // 2), (-n - 1, 2), (0, B))

    def as3(ap, B):
        return ap.rearrange("p (n two b) -> p n two b", two=2, b=B)

    def in_pairs(e, p0, n, body):
        done = 0
        if n >= 4:
            with e.Fori(0, n // 2) as i:
                body(i * 2, p0 % 2)
                body(i * 2 + 1, (p0 + 1) % 2)
            done = n // 2 * 2
        for l in range(done, n):
            body(l, (p0 + l) % 2)

    def with_jobs(e, si, first, body, take, beside=None):
        s, at = STEPS[si], first
        for until, jobs in JOBS_AT[si] + ((s.nf, ()),):
            if jobs and until < s.nf and not beside:
                until += 1
            part_ = lambda l, parity, off=at: body(l + off, parity)
            in_pairs(e, s.pA + at, until - at, part_)
            at = until
            if jobs and until < s.nf and beside:
                beside(until, (s.pA + until) % 2, jobs)
                at += 1
            else:
                take(jobs)

    block = stack.enter_context(nc.Block())

    @block.sync
    def _(sp):
        sp.dma_start(ident[:, :], t["ident"]).then_inc(sem["consts"], 16)
        sp.dma_start(par_rows[0:N_PAR, :], t["params"]).then_inc(sem["params"], 16)
        sp.dma_start(mb_rows[0:N_MOD * KC, :, :], t["mod_b"].rearrange("l (r c) -> r l c", c=P)).then_inc(sem["params"], 16)
        sp.dma_start(xin[:, 0:2, :], t["x"].rearrange("(n p) d -> p n d", p=P)).then_inc(sem["xin_full"], 16)
        sp.dma_start(xin[:, 2:4, :], t["ctx"].rearrange("(n p) d -> p n d", p=P)).then_inc(sem["xin_full"], 16)

        def load(n, slot, src, free=True):
            if free:
                sp.wait_ge(sem["lo_done"], n - (SLOTS - 1))
            dst = w_raw[:, slot, :]
            if len(src.shape) == 3:
                dst = dst.rearrange("p (k c) -> p k c", k=KC)
            sp.dma_start(dst, src).then_inc(raw_full[slot], 16)

        def cols(w, c):
            v = w.rearrange("(k p) c -> p k c", p=P)
            return v[:, :, c * P:(c + 1) * P] if isinstance(c, int) else v[:, :, bass.ds(c * P, P)]

        def rows(w, r):
            return w[r * P:(r + 1) * P, :] if isinstance(r, int) else w[bass.ds(r * P, P), :]

        first = t["mod_w"][0]
        for k in range(KC):
            for m in range(2):
                n = 2 * k + m
                load(n, n % SLOTS, first[k * P:(k + 1) * P, m * D:(m + 1) * D], free=n >= SLOTS)
                if n == SLOTS - 1:
                    sp.dma_start(masks_in[:, :, :], t["masks"]).then_inc(sem["tables"], 16)
                    sp.dma_start(inv_cnt[:, :, :], t["inv_cnt"]).then_inc(sem["tables"], 16)
        for s in STEPS:
            if s.kind == "ffn":
                w1, w3, w2 = t["w1"][s.layer, s.j], t["w3"][s.layer, s.j], t["w2"][s.layer, s.j]

                def up(l, parity):
                    for j, w in enumerate((w1, w3)):
                        load(2 * (s.pA + l) + j, 2 * parity + j, cols(w, l + s.f0))

                def down(l, parity):
                    for j in range(2):
                        load(2 * (s.pB + l) + j, 2 * parity + j, rows(w2, l * 2 + (s.f0 + j)))

                in_pairs(sp, s.pA, s.nf, up)
                if s.pEnd == N_PAIRS:
                    sp.wait_ge(sem["tile_used"], 2 * s.pA + SLOTS)
                    sp.dma_start(g_out[:, :], t["final_g"][None, :].to_broadcast((P, D))).then_inc(sem["g_out_in"], 16)
                in_pairs(sp, s.pB, s.nf // 2, down)
            elif s.kind == "ab":
                tiles = [0, 1]
                q0, v0, f0, b0, g0 = (POOL_TILES + HEADS * i for i in range(5))
                for h in range(HEADS):
                    tiles += [f0 + h, b0 + h, q0 + h, v0 + h]
                tiles += [g0 + h for h in range(HEADS)]
                for i, c in enumerate(tiles):
                    load(2 * s.pA + i, (2 * s.pA + i) % SLOTS, cols(t["ab_w_in"], c))
                    if i == 2 * SLOTS - 1:
                        sp.wait_ge(sem["pool_w"], 1)
                        for g in range(4):
                            r = 64 * (g % 2)
                            sp.dma_start(pw[r:r + 64, g // 2, r:r + 64], t["pool_w"][g]).then_inc(sem["pool_w"], 16)
                for i in range(KC):
                    load(2 * s.pB + i, (2 * s.pB + i) % SLOTS, rows(t["ab_w_out"], i))
            else:
                def columns(l, parity, off=0):
                    for j in range(2):
                        c = l * 2 + (j + KC) if off == 0 else l * 2 + j
                        load(2 * (s.pA + off + l) + j, 2 * parity + j, cols(t["gmlp_w_in"], c))

                for l in range(2):
                    columns(l, (s.pA + l) % 2)
                sp.wait_ge(sem["tile_used"], 2 * s.pA + SLOTS)
                sp.dma_start(ws[:, :, :], t["gmlp_w_s"].rearrange("g p q -> p g q")).then_inc(sem["gm_in"], 16)
                for dst, src in ((ln_g, t["gmlp_ln_g"]), (ln_b, t["gmlp_ln_b"]), (bs, t["gmlp_b_s"])):
                    sp.dma_start(dst[:, :], src[None, :].to_broadcast((P, D))).then_inc(sem["gm_in"], 16)
                for l in range(2, 4):
                    columns(l, (s.pA + l) % 2)
                in_pairs(sp, s.pA + 4, 4, lambda l, parity: columns(l, parity, 4))
                in_pairs(sp, s.pB, 4, lambda l, parity: [
                    load(2 * (s.pB + l) + j, 2 * parity + j, rows(t["gmlp_w_out"], l * 2 + j)) for j in range(2)])
        for n in range(2):
            sp.wait_ge(sem["yo_done"], n + 1)
            sp.dma_start(t["out"][n * P:(n + 1) * P, :], yo[:, n, :]).then_inc(sem["out_done"], 16)
        sp.wait_ge(sem["out_done"], 32)

    @block.gpsimd
    def _(pool):
        pool.wait_ge(sem["act_setup"], 1)
        for n in range(SLOTS):
            pool.wait_ge(sem["hi_done"], n + 1)
            nc.gpsimd.tensor_tensor(w_lo[:, n, :], w_raw[:, n, :], w_hi[:, n, :].bitcast(F32), ALU.subtract).then_inc(sem["lo_done"], 1)
        pool.wait_ge(sem["tile_used"], 2 * FIRST_PAIRS + SLOTS)
        pool.sem_inc(sem["pool_held"], 1)

        def load(w, col, kk):
            src = w.rearrange("(k p) c -> p k c", p=P)[:, 2 * kk:2 * kk + 2]
            src = src[:, :, col] if isinstance(col, slice) else src[:, :, bass.ds(col, D)]
            pool.dma_start(m_raw[:, kk % 2, :, :], src).then_inc(m_full[kk % 2], 16)

        def job(w, col, vec, j, slot):
            seq = j * (2 * KC - 2)
            pool.wait_ge(sem["acc_done"], j + 1)
            pool.sem_inc(sem["pool_held"], 1)
            for kk in range(2):
                load(w, col, kk)
            pool.wait_ge(sem["mod_red"], j + 1)
            n = 0
            for k in range(KC):
                if k % 2 == 0:
                    pool.wait_ge(m_full[(k // 2) % 2], (j * 2 + (k // 4) + 1) * 16)
                    pool.sem_inc(sem["pool_held"], 1)
                src = m_raw[:, (k // 2) % 2, k % 2, :]
                dst = m_acc[:, slot, :] if k == 0 else src
                nc.gpsimd.tensor_scalar(dst, src, silu_c[:, vec * KC + k:vec * KC + k + 1], 0.0,
                                        ALU.mult, ALU.add).then_inc(sem["pool_seq"], 1)
                n += 1
                if k:
                    pool.wait_ge(sem["pool_seq"], seq + n)
                    add = nc.gpsimd.tensor_tensor(m_acc[:, slot, :], m_acc[:, slot, :], src, ALU.add)
                    add.then_inc(sem["pool_seq"] if k < KC - 1 else sem["acc_done"], 1)
                    n += 1
                if k in (1, 3):
                    pool.wait_ge(sem["pool_seq"], seq + n)
                    pool.sem_inc(sem["pool_held"], 1)
                    load(w, col, k // 2 + 2)

        def modules(layer, vecs, m0, n, j0):
            w = t["mod_w"][layer]

            def two(i, j):
                if len(vecs) == 2:
                    for v in vecs:
                        job(w, (i + m0) * D, v, j + v, (j0 + v) % 2)
                else:
                    for r in range(2):
                        job(w, (i * 2 + (m0 + r)) * D, vecs[0], j + r, (j0 + r) % 2)

            rounds = n if len(vecs) == 2 else n // 2
            with pool.Fori(0, rounds) as i:
                two(i, i * 2 + j0)
            if rounds * 2 // len(vecs) < n:
                c = (m0 + n - 1) * D
                job(w, slice(c, c + D), vecs[0], j0 + n - 1, (j0 + n - 1) % 2)

        modules(0, (0, 1), 2, 3, 0)
        modules(0, (0,), 5, 4, 6)

        s = STEPS[AB]
        pool.wait_ge(sem["lo_done"], 2 * (s.pA + 1))

        def split(pair):
            for j in range(2):
                slot = 2 * ((s.pA + pair) % 2) + j
                pool.wait_ge(sem["hi_done"], 2 * (s.pA + pair) + j + 1)
                nc.gpsimd.tensor_tensor(w_lo[:, slot, :], w_raw[:, slot, :], w_hi[:, slot, :].bitcast(F32),
                                        ALU.subtract).then_inc(sem["lo_done"], 1)

        for pair in (1, 2, 3):
            split(pair)
        for h in range(HEADS):
            for L in range(1, LEVELS + 1):
                if L == 1:
                    pool.wait_ge(sem["q_init"], h + 1)
                else:
                    pool.wait_ge(sem["f_merged"], 7 * h + L - 1)
                pool.wait_ge(sem["gathered"], 16 * h + 2 * L)
                q = picked_q(h % 2, 1 << (L - 1))
                nc.gpsimd.tensor_tensor(q, q, other_q(1 << (L - 1)), ALU.mult).then_inc(
                    sem["q_upd"] if L < LEVELS else sem["q_final"], 1)
            split(4 + 2 * h)
            split(5 + 2 * h)
        split(16)
        modules(1, (0,), 0, 9, 10)

    @block.scalar
    def _(act):
        def split(n, slot):
            act.wait_ge(raw_full[slot], raw_count(n, slot))
            act.wait_ge(sem["tile_used"], n + 1)
            nc.scalar.activation(w_hi[:, slot, :], w_raw[:, slot, :], ACT.Copy).then_inc(sem["hi_done"], 1)

        def split_next(l, p0, parity):
            for j in range(2):
                split((l + (p0 + 1)) * 2 + j, 2 * (1 - parity) + j)

        def publish(u, dst, bias=None):
            act.wait_ge(sem["t_done"], u + 1)
            if bias is None:
                nc.scalar.activation(dst, tbuf[:, u % 3, :], ACT.Copy).then_inc(sem["xhi_done"], 1)
            else:
                nc.scalar.activation(dst, tbuf[:, u % 3, :], ACT.Identity, bias=bias).then_inc(sem["xhi_done"], 1)

        def norm_rms(nrm, ev, T, beside=lambda d: None):
            nc.scalar.activation(stat[:, 6:7], eps[:, 0:1], ACT.Sqrt)
            for d in range(KC):
                act.wait_ge(sem["x_upd"], 8 * ev + d + 1)
                if d >= 6:
                    act.wait_ge(sem["sq_used"], SQ_MMS * nrm + d - 5)
                nc.scalar.activation(square_at(d, T), xT[:, d, tok(T)], ACT.Square).then_inc(sem["sq_done"], 1)
                beside(d)
            act.wait_ge(sem["sq_used"], SQ_MMS * (nrm + 1))
            nc.scalar.activation(rms[:, tok(T)], ps[:, ssq_bank(T), tok(T)], ACT.Sqrt, bias=eps[:, 0:1],
                                 scale=1.0 / D).then_inc(sem["rms_done"], 1)

        def norm(nrm, ev, T, shifts, u0, between=None):
            if nrm:
                norm_rms(nrm, ev, T)
            if between:
                between()
            for u, (k, c) in enumerate(norm_units(T)):
                publish(u0 + u, xn_hi[:, k, c * LAT:(c + 1) * LAT], shifts[c][:, k:k + 1])

        act.wait_ge(sem["dve_chain"], DVE_PARAMS)
        nc.scalar.activation(silu_c[:, :], par[:, C_C:C_C + 2 * KC], ACT.Silu).then_inc(sem["act_setup"], 1)
        act.wait_ge(sem["act_setup"], 1)
        nc.scalar.activation(silu_hi[:, :].rearrange("p (k v) -> p v k", v=2),
                             silu_c[:, :].rearrange("p (v k) -> p v k", v=2), ACT.Copy).then_inc(sem["act_setup"], 1)
        act.wait_ge(sem["dve_chain"], DVE_LB)
        nc.scalar.activation(lb_t[:, 0:2, :], lb_t[:, 0:2, :], ACT.Exp).then_inc(sem["act_setup"], 1)
        norm_rms(0, 0, BOTH, lambda d: split(FIRST_SPLITS.index(d), FIRST_SPLITS.index(d)) if d in FIRST_SPLITS else None)
        for l in range(1, FIRST_PAIRS):
            split_next(l, 0, l % 2)
        act.wait_ge(sem["tile_used"], 2 * FIRST_PAIRS + SLOTS)
        nc.scalar.activation(mod_row[:, D:2 * D].rearrange("p (a b) -> p a b", a=2), first_out(1), ACT.Copy).then_inc(sem["row_copied"], 1)
        for si, s in enumerate(STEPS):
            if s.kind == "ffn":
                if not (si == 1):
                    norm(NRM[si], EV_BEFORE[si], s.T, shift_of(mod_cols, s.layer, 6 * s.j, s.T),
                         U0[si])

                def up(l, parity):
                    split_next(l, s.pA, parity)
                    act.wait_ge(sem["tile_used"], (l + s.pA) * 2 + 1 + SLOTS)
                    act.wait_ge(sem["gated"], l + (s.q0 + 1))
                    nc.scalar.activation(act_s[:, parity, tok(s.T)], ps[:, 2 * parity, tok(s.T)],
                                         ACT.Silu).then_inc(sem["silu_done"], 1)
                    act.wait_ge(sem["gated"], l + (s.q0 + 3))
                    nc.scalar.activation(h_at(h_hi, s.T, l), hm[:, parity, tok(s.T)],
                                         ACT.Copy).then_inc(sem["hhi_done"], 1)

                nc.scalar.activation(stat[:, 7:8], eps[:, 0:1], ACT.Silu)
                in_pairs(act, s.pA, s.nf, up)
                n_down = s.nf // 2
                if s.pEnd == N_PAIRS:
                    n_down -= 1
                in_pairs(act, s.pB, n_down, lambda l, parity: split_next(l, s.pB, parity))
            elif s.kind == "ab":
                def split_pair(pair):
                    for j in range(2):
                        split(2 * (s.pA + pair) + j, 2 * ((s.pA + pair) % 2) + j)

                norm(NRM[si], EV_BEFORE[si], BOTH, shift_of(mod_cols, 0, 3, BOTH), U0[si], lambda: split_pair(1))

                def bank(pair, j):
                    return ps[:, 2 * ((s.pA + pair) % 2) + j, :]

                def projected(pair, j):
                    act.wait_ge(sem["tile_used"], 2 * (s.pA + pair) + SLOTS + 1 + j)

                def gathers(h, levels):
                    for L in levels:
                        B = 1 << (L - 1)
                        if L == 1:
                            act.wait_ge(sem["f_done"], 2 * h + 2)
                            if h >= 1:
                                act.wait_ge(sem["lvl_done"], 5 * h)
                        else:
                            act.wait_ge(sem["k_upd"], 7 * h + L - 1)
                        nc.scalar.activation(as3(Kc[:, L, :], B), picked_k(h % 2, B, True), ACT.Copy).then_inc(sem["gathered"], 1)
                        if L == 1:
                            act.wait_ge(sem["q_init"], h + 1)
                        else:
                            act.wait_ge(sem["q_upd"], 7 * h + L - 1)
                        nc.scalar.activation(as3(Qc[:, L, :], B), picked_q(h % 2, B), ACT.Copy).then_inc(sem["gathered"], 1)

                def forget_sigmoid(h, j):
                    if j == 0 and h >= 1:
                        act.wait_ge(sem["f_done"], 2 * h)
                    projected(1 + 2 * h, j)
                    nc.scalar.activation(act_s[:, j, :], bank(1 + 2 * h, j), ACT.Sigmoid).then_inc(sem["sig_done"], 1)

                def gate_sigmoid(g, j):
                    projected(13 + g, j)
                    if g == 0:
                        act.wait_ge(sem[("q_init", "vt_done")[j]], HEADS)
                    else:
                        act.wait_ge(sem["g_done"], 2 * g - 1 + j)
                    nc.scalar.activation(hm[:, j, 0:LAT], bank(13 + g, j)[:, 0:LAT], ACT.Sigmoid).then_inc(sem["g_sig"], 1)

                def outputs(h):
                    act.wait_ge(sem["o_done"], h + 1)
                    nc.scalar.activation(osq, ps[:, 6, 0:LAT], ACT.Square)
                    nc.scalar.activation(Os[:, h, :], ps[:, 6, 0:LAT], ACT.Copy).then_inc(sem["o_copied"], 1)

                def output_rms(h):
                    act.wait_ge(sem["oss_done"], h + 1)
                    if h >= 1:
                        act.wait_ge(sem["o_scaled"], h)
                    nc.scalar.activation(orms, ps[:, 7, 0:LAT], ACT.Sqrt, bias=eps[:, 0:1], scale=1.0 / DH).then_inc(sem["orms_done"], 1)

                projected(0, 1)
                act.wait_ge(sem["pool_w"], 1)
                nc.scalar.activation(rows_of(xp, 1), bank(0, 1)[:, 0:LAT].rearrange("p (r c) -> p r c", r=ROWS), ACT.Copy).then_inc(sem["pool_in"], 1)
                split_pair(2)
                forget_sigmoid(0, 0)
                forget_sigmoid(0, 1)
                split_pair(3)
                for h in range(HEADS):
                    qv = 2 + 2 * h
                    projected(qv, 0)
                    if h >= 1:
                        act.wait_ge(sem["q_init"], h)
                    nc.scalar.activation(hm[:, 0, 0:LAT], bank(qv, 0)[:, 0:LAT], ACT.Sigmoid).then_inc(sem["g_sig"], 1)
                    gathers(h, (1, 2, 3))
                    projected(qv, 1)
                    nc.scalar.activation(hm[:, 1, :], bank(qv, 1), ACT.Copy).then_inc(sem["v_raw"], 1)
                    gathers(h, (4, 5))
                    if h >= 1:
                        outputs(h - 1)
                    gathers(h, (6,))
                    act.wait_ge(sem["vt_done"], h + 1)
                    nc.scalar.activation(Vd[:, h % 2, :, :], bank(qv, 1).rearrange("p (a b) -> p a b", a=4), ACT.Copy).then_inc(sem["v_done"], 1)
                    gathers(h, (7, 8))
                    split_pair(qv + 2)
                    for j in range(2):
                        if h < HEADS - 1:
                            forget_sigmoid(h + 1, j)
                        else:
                            gate_sigmoid(0, j)
                        if j == 0 and h >= 1:
                            output_rms(h - 1)
                    split_pair(qv + 3)
                    act.wait_ge(sem["kt_done"], h + 1)
                    nc.scalar.activation(kT[:, :, :], ps[:, 7, :].rearrange("p (a b) -> p a b", a=4), ACT.Copy).then_inc(sem["kt_copied"], 1)
                    act.wait_ge(sem["s_done"], h + 1)
                    nc.scalar.activation(Sd[:, :, :], ps[:, 7, 0:2 * DH].rearrange("p (a b) -> p a b", a=2), ACT.Copy).then_inc(sem["s_copied"], 1)
                gate_sigmoid(1, 0)
                gate_sigmoid(1, 1)
                split_pair(16)
                outputs(HEADS - 1)
                for c in range(KC):
                    publish(U0[si] + 16 + c, mix_hi[:, c, :])
                    if c == 3:
                        gate_sigmoid(2, 0)
                        output_rms(HEADS - 1)
                        gate_sigmoid(2, 1)
                    if c in MIX_SPLITS:
                        l = MIX_SPLITS.index(c)
                        split_next(l, s.pB, (s.pB + l) % 2)
                split_next(3, s.pB, (s.pB + 3) % 2)
            else:
                norm(NRM[si], EV_BEFORE[si], LAT, shift_of(mod_cols, 1, 3, LAT), U0[si])
                act.wait_ge(sem["ws_t"], 1)
                nc.scalar.activation(wsT[:, :, :], ps[:, 5:7, :].rearrange("p a (g q) -> p (a g) q", q=P), ACT.Copy).then_inc(sem["wsT_done"], 1)

                def gelu(l, j):
                    act.wait_ge(sem["tile_used"], 2 * (s.pA + l) + (j + 1 + SLOTS))
                    if l < 4:
                        if l:
                            act.wait_ge(sem["vt_done"], HEADS + 2 * (l - 1) + j + 1)
                        dst, done = hm[:, j, 0:LAT], sem["v_gelu"]
                    else:
                        dst, done = Ug[:, 2 * (l - 4) + j, :], sem["u_done"]
                    nc.scalar.activation(dst, ps[:, 2 * ((s.pA + l) % 2) + j, 0:LAT], ACT.Gelu_apprx_tanh).then_inc(done, 1)

                def ln_squares(n):
                    act.wait_ge(sem["ln_d"], n + 1)
                    nc.scalar.activation(ps[:, 4:6, :].rearrange("p a b -> p (a b)"), Vt[:, n, :], ACT.Square,
                                         bias=stat[:, 2 + n:3 + n], accum_out=stat[:, 4 + n:5 + n]).then_inc(sem["ln_a"], 1)

                for l in range(8):
                    split_next(l, s.pA, (s.pA + l) % 2)
                    if l == 6:
                        ln_squares(1)
                        act.wait_ge(sem["ln_a"], 2)
                        nc.scalar.activation(stat[:, 0:2], stat[:, 4:6], ACT.Sqrt, bias=eps[:, 0:1], scale=1.0 / D).then_inc(sem["ln_a"], 1)
                    gelu(l, 0)
                    gelu(l, 1)
                    if l == 4:
                        ln_squares(0)
                for g in range(GROUPS):
                    publish(U0[si] + 8 + g, xn_hi[:, g, 0:LAT])
                    if g in OUT_SPLITS:
                        l = OUT_SPLITS.index(g)
                        split_next(l, s.pB, (s.pB + l) % 2)
                split_next(3, s.pB, (s.pB + 3) % 2)
        nc.scalar.activation(stat[:, 6:7], eps[:, 0:1], ACT.Sqrt)
        for n in range(2):
            act.wait_ge(sem["yt_done"], n + 1)
            nc.scalar.activation(ps[:, 4:6, :].rearrange("p a b -> p (a b)"), out_rows(n), ACT.Square,
                                 accum_out=stat[:, 4 + n:5 + n]).then_inc(sem["out_sq"], 1)
            act.wait_ge(sem["out_sq"], n + 1)
            nc.scalar.activation(stat[:, n:n + 1], stat[:, 4 + n:5 + n], ACT.Sqrt, bias=eps[:, 0:1], scale=1.0 / D).then_inc(sem["out_rms"], 1)

    @block.vector
    def _(dve):
        chain = [0]

        def link(ins):
            chain[0] += 1
            ins.then_inc(sem["dve_chain"], 1)
            dve.wait_ge(sem["dve_chain"], chain[0])

        def split(n, slot):
            dve.wait_ge(sem["hi_done"], n + 1)
            nc.vector.tensor_tensor(w_lo[:, slot, :], w_raw[:, slot, :], w_hi[:, slot, :].bitcast(F32),
                                    ALU.subtract).then_inc(sem["lo_done"], 1)

        def split_next(l, p0, parity):
            for j in range(2):
                split((l + (p0 + 1)) * 2 + j, 2 * (1 - parity) + j)

        def slot_read(u):
            if u >= 3:
                dve.wait_ge(sem["xn_done"], u - 2)

        def publish(u, dst_hi, dst_lo, bias=None):
            dve.wait_ge(sem["xhi_done"], u + 1)
            hi = dst_hi.bitcast(F32)
            if bias is None:
                ins = nc.vector.tensor_tensor(dst_lo, tbuf[:, u % 3, :], hi, ALU.subtract)
            else:
                ins = nc.vector.scalar_tensor_tensor(out=dst_lo, in0=tbuf[:, u % 3, :], scalar=bias, in1=hi,
                                                     op0=ALU.add, op1=ALU.subtract)
            ins.then_inc(sem["xn_done"], 1)

        def norm_sums(nrm, T):
            for d in range(SQ_MMS, KC):
                dve.wait_ge(sem["sq_done"], 8 * nrm + d + 1)
                total = square_at(SQ_MMS - 1, T)
                nc.vector.tensor_tensor(total, total, square_at(d, T), ALU.add).then_inc(sem["sq_sum"], 1)
                if d < KC - 1:
                    dve.wait_ge(sem["sq_sum"], (KC - SQ_MMS) * nrm + d - SQ_MMS + 1)

        def norm_rstd(nrm, T, half=None):
            x = tok(T) if half is None else slice(half * LAT, (half + 1) * LAT)
            dve.wait_ge(sem["rms_done"], nrm + 1)
            ins = nc.vector.reciprocal(rstd[:, x], rms[:, x])
            if half != 0:
                ins.then_inc(sem["rstd_done"], 1)
                dve.wait_ge(sem["rstd_done"], nrm + 1)

        def norm(nrm, T, scales, shifts, u0):
            if nrm:
                norm_sums(nrm, T)
                norm_rstd(nrm, T)
            units = norm_units(T)

            def scaled(u):
                k, c = units[u]
                slot_read(u0 + u)
                nc.vector.scalar_tensor_tensor(out=tbuf[:, (u0 + u) % 3, :], in0=xT[:, k, c * LAT:(c + 1) * LAT],
                                               scalar=scales[c][:, k:k + 1], in1=rstd[:, c * LAT:(c + 1) * LAT],
                                               op0=ALU.mult, op1=ALU.mult).then_inc(sem["t_done"], 1)

            scaled(0)
            for u, (k, c) in enumerate(units):
                if u + 1 < len(units):
                    scaled(u + 1)
                cc = slice(c * LAT, (c + 1) * LAT)
                publish(u0 + u, xn_hi[:, k, cc], xn_lo[:, k, cc], shifts[c][:, k:k + 1])

        def finish_mod(row, m, src, n=KC):
            layer = 1 if row == 2 else 0
            dst = mods[:, row, m * KC:(m + 1) * KC]
            ins = nc.vector.tensor_tensor(dst, src, mod_b[:, layer, m * KC:(m + 1) * KC], ALU.add)
            if m % 3 == 1:
                link(ins)
                g = C_NORM + (layer * 3 + m // 3) * KC
                ins = nc.vector.scalar_tensor_tensor(out=dst, in0=dst, scalar=1.0, in1=par[:, g:g + KC],
                                                     op0=ALU.add, op1=ALU.mult)
            elif m in (2, 8):
                link(ins)
                ins = nc.vector.tensor_scalar(dst, dst, 0.5, None, ALU.mult)
            return ins

        def take_jobs(jobs):
            if jobs:
                dve.wait_ge(sem["mod_red"], jobs[-1] + 3)
            for j in jobs:
                layer, vec, m = JOBS[j]
                finish_mod(2 if layer else vec, m, ps[:, 7, (j % 2) * KC:(j % 2 + 1) * KC]).then_inc(sem["mod_fin"], 1)
                dve.wait_ge(sem["mod_fin"], j + 2)

        def evict(ev, T, tiles, gates):
            per_bank = BOTH // T
            for d in range(KC):
                if d == KC - per_bank:
                    dve.wait_ge(sem["tile_used"], tiles + SLOTS)
                elif d % per_bank == 0:
                    dve.wait_ge(sem["y_ready"], Y0[ev] + d // per_bank + 1)
                y = y_at(T, d)
                for c in range(T // LAT):
                    cc = slice(c * LAT, (c + 1) * LAT)
                    ins = nc.vector.scalar_tensor_tensor(out=xT[:, d, cc], in0=y if T == LAT else y[:, cc],
                                                         scalar=gates[c][:, d:d + 1], in1=xT[:, d, cc],
                                                         op0=ALU.mult, op1=ALU.add)
                ins.then_inc(sem["x_upd"], 1)

        nc.vector.memset(ones[:, :], 1.0)
        link(nc.vector.memset(eps[:, :], EPS))
        for s_, n_ in ((sem["tile_used"], SLOTS), (sem["gated"], 2), (sem["mod_red"], 2), (sem["acc_done"], 1)):
            dve.sem_inc(s_, n_)
        dve.wait_ge(sem["turned_in"], 1)
        nc.vector.tensor_copy(par[:, :], ps[:, 0, 0:N_PAR])
        link(nc.vector.tensor_copy(mod_b[:, :, :], ps[:, 0, P:P + 2 * P].rearrange("p (a b) -> p a b", a=2)[:, :, 0:N_MOD * KC]))
        assert chain[0] == DVE_PARAMS
        L0, L1 = par[:, C_LB:C_LB + 12], par[:, C_LB + 12:C_LB + 24]
        link(nc.vector.tensor_tensor(lb_t[:, 2, :], L0, L1, ALU.max))
        nc.vector.tensor_tensor(lb_t[:, 0, :], L0, lb_t[:, 2, :], ALU.subtract)
        link(nc.vector.tensor_tensor(lb_t[:, 1, :], L1, lb_t[:, 2, :], ALU.subtract))
        assert chain[0] == DVE_LB
        dve.wait_ge(sem["act_setup"], 2)
        nc.vector.tensor_tensor(silu_lo[:, :].rearrange("p (k v) -> p v k", v=2), silu_c[:, :].rearrange("p (v k) -> p v k", v=2),
                                silu_hi[:, :].bitcast(F32).rearrange("p (k v) -> p v k", v=2), ALU.subtract).then_inc(sem["silu_split"], 1)
        for k in range(KC):
            dve.wait_ge(sem["turned_in"], 2 + k)
            nc.vector.tensor_copy(xT[:, k, :], ps[:, X_BANKS[k % 4], :]).then_inc(sem["x_upd"], 1)
        norm_sums(0, BOTH)
        dve.wait_ge(sem["act_setup"], 3)
        link(nc.vector.tensor_tensor(lb_t[:, 2, :], lb_t[:, 0, :], lb_t[:, 1, :], ALU.add))
        link(nc.vector.reciprocal(lb_t[:, 3, :], lb_t[:, 2, :]))
        nc.vector.tensor_tensor(one_lb[:, :], lb_t[:, 1, :], lb_t[:, 3, :], ALU.mult)
        link(nc.vector.tensor_tensor(lb[:, :], lb_t[:, 0, :], lb_t[:, 3, :], ALU.mult))
        norm_rstd(0, BOTH, 0)
        dve.wait_ge(sem["lo_done"], SLOTS)
        for l in range(1, FIRST_PAIRS - 1):
            split_next(l, 0, l % 2)
            if l == 2:
                norm_rstd(0, BOTH, 1)
            if l == 4:
                dve.wait_ge(sem["tables"], 32)
                nc.vector.tensor_copy(masks[:, :, :], masks_in[:, :, :])
        split(2 * FIRST_PAIRS, 0)
        dve.wait_ge(sem["tile_used"], 2 * FIRST_PAIRS + SLOTS)
        nc.vector.tensor_copy(mod_row[:, 0:D].rearrange("p (a b) -> p a b", a=2), first_out(0)).then_inc(sem["row_copied"], 1)
        split(2 * FIRST_PAIRS + 1, 1)
        dve.wait_ge(sem["first_turned"], 1)
        sums = ps[:, 5, 0:4 * KC].rearrange("p (c two) -> p two c", two=2)
        for m in range(2):
            for v in range(2):
                last = finish_mod(v, m, sums[:, v, m * KC:(m + 1) * KC])
                if (m, v) != (1, 1):
                    link(last)
        last.then_inc(sem["mod_fin"], 1)
        dve.wait_ge(sem["mod_fin"], 1)

        for si, s in enumerate(STEPS):
            if s.kind == "ffn":
                m0 = 0 if s.j == 0 else 6
                if si != 1:
                    norm(NRM[si], s.T, shift_of(mod_cols, s.layer, m0 + 1, s.T), shift_of(mod_cols, s.layer, m0, s.T), U0[si])

                take_jobs(JOBS_BEFORE[si])

                def up(l, parity):
                    split_next(l, s.pA, parity)
                    dve.wait_ge(sem["silu_done"], l + (s.q0 + 1))
                    dve.wait_ge(sem["tile_used"], (l + s.pA) * 2 + 2 + SLOTS)
                    dve.wait_ge(sem["lo_done"], (l + s.pA) * 2 + 2)
                    nc.vector.tensor_tensor(hm[:, parity, tok(s.T)], act_s[:, parity, tok(s.T)], ps[:, 2 * parity + 1, tok(s.T)],
                                            ALU.mult).then_inc(sem["gated"], 1)
                    dve.wait_ge(sem["hhi_done"], l + (s.q0 + 1))
                    nc.vector.tensor_tensor(h_at(h_lo, s.T, l), hm[:, parity, tok(s.T)], h_at(h_hi, s.T, l).bitcast(F32),
                                            ALU.subtract).then_inc(sem["hlo_done"], 1)

                with_jobs(dve, si, 0, up, take_jobs)
                n_down = s.nf // 2 - (s.pEnd == N_PAIRS)
                in_pairs(dve, s.pB, n_down, lambda l, parity: split_next(l, s.pB, parity))
                evict(EV[si], s.T, 2 * s.pEnd, shift_of(mod_cols, s.layer, m0 + 2, s.T))
            elif s.kind == "ab":
                norm(NRM[si], BOTH, shift_of(mod_cols, 0, 4, BOTH), shift_of(mod_cols, 0, 3, BOTH), U0[si])
                take_jobs(JOBS_BEFORE[si])
                nc.vector.memset(xp[:, :, :], 0.0)
                nc.vector.memset(pw[:, :, :], 0.0).then_inc(sem["pool_w"], 1)

                def bank(pair, j):
                    return ps[:, 2 * ((s.pA + pair) % 2) + j, :]

                def queries(h):
                    hp = h % 2
                    dve.wait_ge(sem["g_sig"], h + 1)
                    if h >= 1:
                        dve.wait_ge(sem["lvl_done"], 5 * h)
                    if h >= 2:
                        dve.wait_ge(sem["o_done"], h - 1)
                    nc.vector.scalar_tensor_tensor(out=Qc[:, 0, :], in0=bank(2 + 2 * h, 0)[:, 0:LAT], scalar=float(DH) ** -0.5,
                                                   in1=hm[:, 0, 0:LAT], op0=ALU.mult, op1=ALU.mult).then_inc(sem["q_read"], 1)
                    dve.wait_ge(sem["f_done"], 2 * h + 2)
                    nc.vector.tensor_tensor(Kc[:, 0, :], Kd[:, hp, 0, 0:LAT], Kd[:, hp, 1, 0:LAT], ALU.add).then_inc(sem["kq0_done"], 1)
                    dve.wait_ge(sem["q_read"], h + 1)
                    nc.vector.tensor_tensor(Qd[:, hp, 0, :], Qc[:, 0, :], Fg[:, 1, 0:LAT], ALU.mult)
                    nc.vector.tensor_tensor(Qd[:, hp, 1, :], Qc[:, 0, :], Fg[:, 0, 0:LAT], ALU.mult).then_inc(sem["q_init"], 1)

                def updates(h):
                    hp = h % 2
                    if h >= 1:
                        dve.wait_ge(sem["q_final"], h)
                    for L in range(1, LEVELS):
                        B = 1 << (L - 1)
                        n = BOTH // B
                        buf, width, at = blocks(B)
                        left, right = (ap3(buf, width, at + o, (n, 2), (2, n // 2)) for o in (0, 1))
                        nc.vector.tensor_tensor(Fb[:, block_at(2 * B):block_at(2 * B) + n].rearrange("p (a b) -> p a b", a=2),
                                                left, right, ALU.mult).then_inc(sem["f_merged"], 1)
                        dve.wait_ge(sem["gathered"], 16 * h + 2 * L - 1)
                        if L == 1:
                            dve.wait_ge(sem["kq0_done"], h + 1)
                        k = picked_k(hp, B, False)
                        nc.vector.tensor_tensor(k, k, other_k(B), ALU.mult).then_inc(sem["k_upd"], 1)
                        dve.wait_ge(sem["f_merged"], 7 * h + L)
                    dve.wait_ge(sem["gathered"], 16 * h + 15)
                    dve.wait_ge(sem["k_upd"], 7 * h + 7)
                    k = picked_k(hp, P, False, True)
                    nc.vector.tensor_tensor(k, k, other_k(P, True), ALU.mult).then_inc(sem["k_final"], 1)

                def forget(h, j):
                    hp, c = h % 2, j * HEADS + h
                    dve.wait_ge(sem["sig_done"], 2 * h + j + 1)
                    if h >= 1:
                        dve.wait_ge(sem["q_upd"], 7 * h)
                    link(nc.vector.tensor_scalar(Fg[:, j, :], act_s[:, j, :], one_lb[:, c:c + 1], lb[:, c:c + 1],
                                                 ALU.mult, ALU.add))
                    if j == 0 and h >= 2:
                        dve.wait_ge(sem["kt_done"], h - 1)
                    nc.vector.tensor_scalar(Kd[:, hp, j, :], Fg[:, j, :], -1.0, 1.0, ALU.mult, ALU.add).then_inc(sem["f_done"], 1)

                def gate(g, j):
                    dve.wait_ge(sem["g_sig"], HEADS + 2 * g + j + 1)
                    nc.vector.tensor_tensor(Gs[:, 2 * g + j, :], bank(13 + g, j)[:, 0:LAT], hm[:, j, 0:LAT], ALU.mult).then_inc(sem["g_done"], 1)

                def scores(h, groups):
                    for b in groups:
                        i = 5 * h + b
                        dve.wait_ge(sem["lvl_done"], i + 1)
                        if b == 0 and h >= 1:
                            dve.wait_ge(sem["o_done"], h)
                        if b == 4:
                            nc.vector.tensor_copy(Ax[:, :, :], ps[:, 4 + i % 2, 0:2 * P].rearrange("p (a b) -> p a b", a=2)).then_inc(sem["cp_done"], 1)
                            continue
                        for L in (2 * b, 2 * b + 1):
                            src = ps[:, 4 + i % 2, (L % 2) * 2 * P:(L % 2) * 2 * P + 2 * P].rearrange("p (a b) -> p a b", a=2)
                            if L == 0:
                                ins = nc.vector.tensor_copy(Am[:, :, :], src)
                            else:
                                mask = ap3(masks, LEVELS * P, L * P, (0, 2), (1, P))
                                ins = nc.vector.copy_predicated(Am[:, :, :], mask, src)
                            if L % 2 == 0:
                                link(ins)
                        ins.then_inc(sem["cp_done"], 1)
                        dve.wait_ge(sem["cp_done"], i + 1)

                def scaled_output(h):
                    dve.wait_ge(sem["orms_done"], h + 1)
                    link(nc.vector.reciprocal(orstd, orms))
                    dve.wait_ge(sem["o_copied"], h + 1)
                    nc.vector.scalar_tensor_tensor(out=Os[:, h, :], in0=Os[:, h, :], scalar=par[:, C_HG + h:C_HG + h + 1],
                                                   in1=orstd, op0=ALU.mult, op1=ALU.mult).then_inc(sem["o_scaled"], 1)

                dve.wait_ge(sem["tile_used"], 2 * s.pA + SLOTS + 1)
                dve.wait_ge(sem["pool_w"], 1)
                nc.vector.tensor_copy(rows_of(xp, 0), bank(0, 0)[:, 0:LAT].rearrange("p (r c) -> p r c", r=ROWS)).then_inc(sem["pool_in"], 1)
                dve.wait_ge(sem["pool_in"], 2)
                pool_windows(nc, dve, link, xp, xs, py, inv_cnt, sem)
                forget(0, 0)
                forget(0, 1)
                for h in range(HEADS):
                    queries(h)
                    updates(h)
                    if h == 0:
                        dve.wait_ge(sem["pm_done"], 1)
                        nc.vector.tensor_copy(py[:, :, :], ps[:, 6, :].rearrange("p (a b) -> p a b", a=2)).then_inc(sem["pooled"], 1)
                    if h < HEADS - 1:
                        forget(h + 1, 0)
                    else:
                        gate(0, 0)
                    scores(h, (0, 1))
                    if h >= 1:
                        scaled_output(h - 1)
                    if h < HEADS - 1:
                        forget(h + 1, 1)
                    else:
                        gate(0, 1)
                    scores(h, (2, 3, 4))
                gate(1, 0)
                gate(1, 1)
                u0 = U0[si] + 16

                def mixed(c):
                    slot_read(u0 + c)
                    if c < POOL_TILES:
                        ins = nc.vector.tensor_scalar(tbuf[:, (u0 + c) % 3, :], py[:, c, :], par[:, C_PS + c:C_PS + c + 1], None, ALU.mult)
                    else:
                        if c % 2 == 0:
                            dve.wait_ge(sem["g_done"], c)
                        dve.wait_ge(sem["o_scaled"], c - 1)
                        ins = nc.vector.tensor_tensor(tbuf[:, (u0 + c) % 3, :], Os[:, c - 2, :], Gs[:, c - 2, :], ALU.mult)
                    ins.then_inc(sem["t_done"], 1)

                mixed(0)
                for c in range(KC):
                    if c == KC - 2:
                        scaled_output(HEADS - 1)
                    if c + 1 < KC:
                        mixed(c + 1)
                    publish(u0 + c, mix_hi[:, c, :], mix_lo[:, c, :])
                    if c == 3:
                        gate(2, 0)
                        gate(2, 1)
                    if c in MIX_SPLITS:
                        l = MIX_SPLITS.index(c)
                        if l == 0:
                            dve.wait_ge(sem["lo_done"], 2 * (s.pB + 1))
                        split_next(l, s.pB, (s.pB + l) % 2)
                split_next(3, s.pB, (s.pB + 3) % 2)
                evict(EV[si], LAT, 2 * s.pEnd, [mod_cols(0, 0, 5)])
            else:
                norm(NRM[si], LAT, [mod_cols(1, 0, 4)], [mod_cols(1, 0, 3)], U0[si])
                take_jobs(JOBS_BEFORE[si])
                def turned(l):
                    for j in range(2):
                        dve.wait_ge(sem["vt_done"], HEADS + 2 * l + j + 1)
                        g = 2 * l + j
                        nc.vector.tensor_copy(Vt[:, :, g * P:(g + 1) * P],
                                              ps[:, 2 * ((s.pA + l) % 2) + j, 0:LAT].rearrange("p (a b) -> p a b", a=2)).then_inc(sem["v_copied"], 1)

                def mean(n):
                    link(nc.vector.tensor_reduce(stat[:, n:n + 1], Vt[:, n, :], AX.X, ALU.add))
                    nc.vector.tensor_scalar(stat[:, 2 + n:3 + n], stat[:, n:n + 1], -1.0 / D, None, ALU.mult).then_inc(sem["ln_d"], 1)

                def centred(n):
                    dve.wait_ge(sem["ln_a"], n + 1)
                    dve.wait_ge(sem["ln_d"], n + 1)
                    nc.vector.scalar_tensor_tensor(out=Vt[:, n, :], in0=Vt[:, n, :], scalar=stat[:, 2 + n:3 + n], in1=ln_g[:, :],
                                                   op0=ALU.add, op1=ALU.mult).then_inc(sem["ln_c"], 1)

                def normalised(n):
                    dve.wait_ge(sem["ln_c"], n + 1)
                    nc.vector.scalar_tensor_tensor(out=Vt[:, n, :], in0=Vt[:, n, :], scalar=stat[:, 4 + n:5 + n], in1=ln_b[:, :],
                                                   op0=ALU.mult, op1=ALU.add).then_inc(sem["ln_done"], 1)

                for l in range(8):
                    split_next(l, s.pA, (s.pA + l) % 2)
                    if 1 <= l <= 4:
                        turned(l - 1)
                    if l == 4:
                        dve.wait_ge(sem["v_copied"], 8)
                        dve.wait_ge(sem["gm_in"], 64)
                        mean(0)
                    if l == 5:
                        mean(1)
                        centred(0)
                    if l == 6:
                        centred(1)
                        dve.wait_ge(sem["ln_a"], 3)
                        link(nc.vector.reciprocal(stat[:, 4:6], stat[:, 0:2]))
                        normalised(0)
                        normalised(1)
                u0 = U0[si] + 8

                def gated(g):
                    dve.wait_ge(sem["sv_done"], g + 1)
                    slot_read(u0 + g)
                    bias = ap3(bs, D, g * P, (0, 2), (1, P))
                    link(nc.vector.tensor_tensor(sv[:, g % 2, :].rearrange("p (a b) -> p a b", a=2),
                                                 ps[:, g % 4, 0:LAT].rearrange("p (a b) -> p a b", a=2), bias, ALU.add))
                    nc.vector.tensor_tensor(tbuf[:, (u0 + g) % 3, :], sv[:, g % 2, :], Ug[:, g, :], ALU.mult).then_inc(sem["t_done"], 1)

                dve.wait_ge(sem["tile_used"], 2 * s.pB + SLOTS)
                gated(0)
                for g in range(GROUPS):
                    if g + 1 < GROUPS:
                        gated(g + 1)
                    publish(u0 + g, xn_hi[:, g, 0:LAT], xn_lo[:, g, 0:LAT])
                    if g in OUT_SPLITS:
                        l = OUT_SPLITS.index(g)
                        split_next(l, s.pB, (s.pB + l) % 2)
                split_next(3, s.pB, (s.pB + 3) % 2)
                evict(EV[si], LAT, 2 * s.pEnd, [mod_cols(1, 0, 5)])
        dve.wait_ge(sem["g_out_in"], 16)
        for n in range(2):
            dve.wait_ge(sem["out_rms"], n + 1)
            link(nc.vector.reciprocal(stat[:, 2 + n:3 + n], stat[:, n:n + 1]))
            nc.vector.scalar_tensor_tensor(out=yo[:, n, :], in0=out_rows(n), scalar=stat[:, 2 + n:3 + n], in1=g_out[:, :],
                                           op0=ALU.mult, op1=ALU.mult).then_inc(sem["yo_done"], 1)

    @block.tensor
    def _(pe):
        def product(out, st_hi, st_lo, mv_hi, mv_lo, start, stop, shared=False):
            nc.tensor.matmul(out, st_lo, mv_hi, start=start, stop=False, skip_group_check=shared)
            nc.tensor.matmul(out, st_hi, mv_lo, start=False, stop=False, skip_group_check=shared)
            return nc.tensor.matmul(out, st_hi, mv_hi, start=False, stop=stop, skip_group_check=shared)

        def tile_ready(n):
            pe.wait_ge(sem["lo_done"], n + 1)

        def project(n, slot, T, job=None):
            tile_ready(n)
            for k in range(KC):
                w = slice(k * P, (k + 1) * P)
                last = product(ps[:, slot, 0:T], w_hi[:, slot, w], w_lo[:, slot, w],
                               xn_hi[:, k, 0:T], xn_lo[:, k, 0:T], k == 0, k == KC - 1)
                if job is not None and k < KC - 1:
                    job_column(job, k)
            last.then_inc(sem["tile_used"], 1)
            if job is not None:
                job_column(job, KC - 1).then_inc(sem["mod_red"], 1)

        def project_first(n0, widths, xn0, per_chunk):
            for i in range(len(widths)):
                tile_ready(n0 + i)
            for k in range(KC):
                pe.wait_ge(sem["xn_done"], xn0 + (k + 1) * per_chunk)
                for i, T in enumerate(widths):
                    slot, w = (n0 + i) % SLOTS, slice(k * P, (k + 1) * P)
                    last = product(ps[:, slot, 0:T], w_hi[:, slot, w], w_lo[:, slot, w],
                                   xn_hi[:, k, 0:T], xn_lo[:, k, 0:T], k == 0, k == KC - 1, shared=True)
                    if k == KC - 1:
                        last.then_inc(sem["tile_used"], 1)

        def down(n, slot, T, hi, lo, start, stop):
            tile_ready(n)
            per_bank = BOTH // T
            for d in range(KC):
                w = slice(d * P, (d + 1) * P)
                last = product(y_at(T, d), w_hi[:, slot, w], w_lo[:, slot, w], hi, lo,
                               start and d % per_bank == 0, stop, shared=True)
                if stop and d % per_bank == per_bank - 1 and d < KC - 1:
                    last.then_inc(sem["y_ready"], 1)
            last.then_inc(sem["tile_used"], 1)

        def norm(nrm, T):
            for d in range(SQ_MMS):
                if d < SQ_MMS - 1:
                    pe.wait_ge(sem["sq_done"], 8 * nrm + d + 1)
                else:
                    pe.wait_ge(sem["sq_sum"], (KC - SQ_MMS) * (nrm + 1))
                nc.tensor.matmul(ps[:, ssq_bank(T), tok(T)], ones[:, :], square_at(d, T),
                                 start=(d == 0), stop=(d == SQ_MMS - 1)).then_inc(sem["sq_used"], 1)

        def take_jobs(jobs):
            if jobs:
                pe.wait_ge(sem["mod_fin"], jobs[0] + 1)
            for j in jobs:
                pe.wait_ge(sem["acc_done"], j + 2)
                for c in range(KC):
                    mm = job_column(j, c)
                mm.then_inc(sem["mod_red"], 1)

        def job_column(j, c):
            col = (j % 2) * KC + c
            return nc.tensor.matmul(ps[:, 7, col:col + 1], m_acc[:, j % 2, c * P:(c + 1) * P], ones[:, 0:1],
                                    start=True, stop=True, skip_group_check=True)

        pe.wait_ge(sem["consts"], 16)
        pe.wait_ge(sem["params"], 32)
        pe.wait_ge(sem["dve_chain"], 1)
        nc.tensor.transpose(ps[:, 0, 0:N_PAR], par_rows[0:N_PAR, :], ident[0:N_PAR, 0:N_PAR])
        R = N_MOD * KC
        for l in range(2):
            mm = nc.tensor.transpose(ps[:, 0, P + l * P:P + l * P + R], mb_rows[0:R, l, :], ident[0:R, 0:R])
        mm.then_inc(sem["turned_in"], 1)
        pe.wait_ge(sem["xin_full"], 32)
        for k in range(KC):
            if k >= 4:
                pe.wait_ge(sem["x_upd"], k - 3)
            for n in range(4):
                mm = nc.tensor.transpose(ps[:, X_BANKS[k % 4], n * P:(n + 1) * P], xin[:, n, k * P:(k + 1) * P], ident[:, :])
            mm.then_inc(sem["turned_in"], 1)
        norm(0, BOTH)
        pe.wait_ge(sem["silu_split"], 1)
        for k in range(KC):
            for m in range(2):
                n = 2 * k + m
                tile_ready(n)
                for half in range(2):
                    c = slice(half * 512, half * 512 + 512)
                    last = product(first_out(m)[:, half, :], silu_hi[:, 2 * k:2 * k + 2], silu_lo[:, 2 * k:2 * k + 2],
                                   w_hi[:, n % SLOTS, c], w_lo[:, n % SLOTS, c], k == 0, k == KC - 1)
                last.then_inc(sem["tile_used"], 1)
        pe.wait_ge(sem["row_copied"], 2)
        for c in range(2 * KC):
            mm = nc.tensor.transpose(ps[:, 5, 2 * c:2 * c + 2], mod_row[:, c * P:(c + 1) * P], ident[0:2, 0:2])
        mm.then_inc(sem["first_turned"], 1)

        for si, s in enumerate(STEPS):
            if s.kind == "ffn":
                if si > 1:
                    norm(NRM[si], s.T)
                    take_jobs(JOBS_BEFORE[si])
                elif si == 1:
                    pe.wait_ge(sem["x_upd"], 8 * EV[0] + 4)
                    take_jobs(JOBS_BEFORE[si])
                    pe.wait_ge(sem["x_upd"], 8 * EV[0] + 8)
                pe.wait_ge(sem["gated"], s.q0 + 2)
                par0 = s.pA % 2
                if si == 1:
                    for j in range(2):
                        project(2 * s.pA + j, 2 * par0 + j, s.T)
                else:
                    project_first(2 * s.pA, (s.T, s.T), U0[si], s.T // LAT)

                def up(l, parity):
                    pe.wait_ge(sem["gated"], l + (s.q0 + 1))
                    for j in range(2):
                        project((l + s.pA) * 2 + j, 2 * parity + j, s.T)

                def up_with_jobs(l, parity, jobs):
                    pe.wait_ge(sem["gated"], l + (s.q0 + 1))
                    pe.wait_ge(sem["mod_fin"], jobs[0] + 1)
                    for i, j in enumerate(jobs):
                        pe.wait_ge(sem["acc_done"], j + 2)
                        project((l + s.pA) * 2 + i, 2 * parity + i, s.T, j)

                with_jobs(pe, si, 1, up, take_jobs, up_with_jobs)
                pe.wait_ge(sem["mod_fin"], jobs_taken(si) + 1)
                if s.T == BOTH:
                    pe.wait_ge(sem["gated"], s.q0 + s.nf + 2)

                def add(l, parity, start=False, stop=False, skip=0):
                    for j in range(2):
                        f = (l + skip) * 2 + j
                        pe.wait_ge(sem["hlo_done"], f + (s.q0 + 1))
                        down((l + (s.pB + skip)) * 2 + j, 2 * parity + j, s.T, h_at(h_hi, s.T, f), h_at(h_lo, s.T, f),
                             start and j == 0, stop and j == 1)

                n = s.nf // 2
                add(0, s.pB % 2, start=True)
                in_pairs(pe, s.pB + 1, n - 2, lambda l, parity: add(l, parity, skip=1))
                add(n - 1, (s.pB + n - 1) % 2, stop=True)
            elif s.kind == "ab":
                norm(NRM[si], BOTH)
                take_jobs(JOBS_BEFORE[si])

                def banks_free(pair):
                    if pair == 2:
                        pe.wait_ge(sem["pool_in"], 2)
                    elif pair == 15:
                        pe.wait_ge(sem["g_done"], 2)
                    elif pair % 2:
                        pe.wait_ge(sem["sig_done"], pair - 1)
                    elif pair:
                        pe.wait_ge(sem["q_read"], pair // 2 - 1)
                        pe.wait_ge(sem["v_done"], pair // 2 - 1)

                def project_one(pair, j, T):
                    project(2 * (s.pA + pair) + j, 2 * ((s.pA + pair) % 2) + j, T)

                def levels(h, groups):
                    for b in groups:
                        i = 5 * h + b
                        if i >= 2:
                            pe.wait_ge(sem["cp_done"], i - 1)
                        if b == 0:
                            pe.wait_ge(sem["kq0_done"], h + 1)
                        pe.wait_ge(sem["gathered"], 16 * h + min(4 * b + 2, 16))
                        if b < 4:
                            for L in (2 * b, 2 * b + 1):
                                for n in range(2):
                                    at = (L % 2) * 2 * P + n * P
                                    x = slice(n * P, (n + 1) * P)
                                    mm = nc.tensor.matmul(ps[:, 4 + i % 2, at:at + P], Kc[:, L, x], Qc[:, L, x], start=True, stop=True)
                        else:
                            for n in range(2):
                                mm = nc.tensor.matmul(ps[:, 4 + i % 2, n * P:(n + 1) * P], Kc[:, LEVELS, n * P:(n + 1) * P],
                                                      Qc[:, LEVELS, (1 - n) * P:(2 - n) * P], start=True, stop=True)
                        mm.then_inc(sem["lvl_done"], 1)

                def turned_keys(h):
                    pe.wait_ge(sem["k_final"], h + 1)
                    if h >= 1:
                        pe.wait_ge(sem["orms_done"], h)
                    else:
                        pe.wait_ge(sem["mod_fin"], jobs_taken(si) + 1)
                    for d in range(2):
                        for n in range(2):
                            mm = nc.tensor.transpose(ps[:, 7, (2 * d + n) * P:(2 * d + n + 1) * P],
                                                     Kd[:, h % 2, d, LAT + n * P:LAT + (n + 1) * P], ident[:, :])
                    mm.then_inc(sem["kt_done"], 1)

                def states(h):
                    pe.wait_ge(sem["kt_copied"], h + 1)
                    pe.wait_ge(sem["v_done"], h + 1)
                    for d in range(2):
                        for n in range(2):
                            mm = nc.tensor.matmul(ps[:, 7, d * DH:(d + 1) * DH], kT[:, 2 * d + n, :], Vd[:, h % 2, 2 + n, :],
                                                  start=(n == 0), stop=(n == 1))
                    mm.then_inc(sem["s_done"], 1)

                def outputs(h):
                    hp = h % 2
                    pe.wait_ge(sem["s_copied"], h + 1)
                    pe.wait_ge(sem["q_final"], h + 1)
                    pe.wait_ge(sem["cp_done"], 5 * h + 5)
                    if h >= 1:
                        pe.wait_ge(sem["o_copied"], h)
                    else:
                        pe.wait_ge(sem["pooled"], 1)
                    o = ps[:, 6, :]
                    nc.tensor.matmul(o[:, 0:LAT], Sd[:, 0, :], Qd[:, hp, 1, :], start=True, stop=False, skip_group_check=True)
                    nc.tensor.matmul(o[:, 0:LAT], Sd[:, 1, :], Qd[:, hp, 0, :], start=False, stop=False, skip_group_check=True)
                    for n in range(2):
                        x, y = slice(n * P, (n + 1) * P), slice((1 - n) * P, (2 - n) * P)
                        nc.tensor.matmul(o[:, x], Vd[:, hp, n, :], Am[:, n, :], start=False, stop=False, skip_group_check=True)
                        mm = nc.tensor.matmul(o[:, y], Vd[:, hp, n, :], Ax[:, n, :], start=False, stop=(n == 1), skip_group_check=True)
                    mm.then_inc(sem["o_done"], 1)

                def output_squares(h):
                    pe.wait_ge(sem["o_copied"], h + 1)
                    nc.tensor.matmul(ps[:, 7, 0:LAT], ones[:, :], osq, start=True, stop=True).then_inc(sem["oss_done"], 1)

                project_first(2 * s.pA, (LAT, LAT, BOTH), U0[si], 2)
                project_one(1, 1, BOTH)
                for h in range(HEADS):
                    qv = 2 + 2 * h
                    banks_free(qv)
                    project_one(qv, 0, LAT)
                    project_one(qv, 1, BOTH)
                    if h == 0:
                        pe.wait_ge(sem["py_done"], 1)
                        pe.wait_ge(sem["pool_w"], 1 + 64)
                        for c in range(POOL_TILES):
                            mm = nc.tensor.matmul(ps[:, 6, c * LAT:(c + 1) * LAT], pw[:, c, :], py[:, c, :], start=True, stop=True)
                        mm.then_inc(sem["pm_done"], 1)
                    else:
                        outputs(h - 1)
                    pe.wait_ge(sem["v_raw"], h + 1)
                    for n in range(4):
                        mm = nc.tensor.transpose(ps[:, 2 * ((s.pA + qv) % 2) + 1, n * P:(n + 1) * P], hm[:, 1, n * P:(n + 1) * P], ident[:, :])
                    mm.then_inc(sem["vt_done"], 1)
                    T = BOTH if h < HEADS - 1 else LAT
                    banks_free(qv + 1)
                    project_one(qv + 1, 0, T)
                    levels(h, (0, 1))
                    if h >= 1:
                        output_squares(h - 1)
                    project_one(qv + 1, 1, T)
                    levels(h, (2, 3))
                    turned_keys(h)
                    levels(h, (4,))
                    states(h)
                banks_free(14)
                project_one(14, 0, LAT)
                project_one(14, 1, LAT)
                outputs(HEADS - 1)
                banks_free(15)
                project_one(15, 0, LAT)
                output_squares(HEADS - 1)
                project_one(15, 1, LAT)
                pe.wait_ge(sem["orms_done"], HEADS)
                for c in range(KC):
                    pe.wait_ge(sem["xn_done"], U0[si] + 16 + c + 1)
                    down(2 * s.pB + c, (2 * s.pB + c) % SLOTS, LAT, mix_hi[:, c, :], mix_lo[:, c, :], c == 0, c == KC - 1)
            else:
                norm(NRM[si], LAT)
                take_jobs(JOBS_BEFORE[si])
                pe.wait_ge(sem["gm_in"], 64)
                for g in range(GROUPS):
                    mm = nc.tensor.transpose(ps[:, 5 + g // 4, (g % 4) * P:(g % 4 + 1) * P], ws[:, g, :], ident[:, :])
                mm.then_inc(sem["ws_t"], 1)

                def turn(l):
                    for j in range(2):
                        pe.wait_ge(sem["v_gelu"], 2 * l + j + 1)
                        for n in range(2):
                            mm = nc.tensor.transpose(ps[:, 2 * ((s.pA + l) % 2) + j, n * P:(n + 1) * P], hm[:, j, n * P:(n + 1) * P], ident[:, :])
                        mm.then_inc(sem["vt_done"], 1)

                project_first(2 * s.pA, (LAT, LAT), U0[si], 1)
                for l in range(1, 8):
                    for j in range(2):
                        if 2 <= l < 6:
                            pe.wait_ge(sem["v_copied"], 2 * (l - 2) + j + 1)
                        elif l >= 6:
                            pe.wait_ge(sem["u_done"], 2 * (l - 6) + j + 1)
                        project(2 * (s.pA + l) + j, 2 * ((s.pA + l) % 2) + j, LAT)
                    if 1 <= l <= 4:
                        turn(l - 1)

                def spatial(g):
                    if g < 4:
                        pe.wait_ge(sem["u_done"], 8)
                    else:
                        pe.wait_ge(sem["t_done"], U0[si] + 8 + g - 3)
                    for n in range(2):
                        mm = nc.tensor.matmul(ps[:, g % 4, n * P:(n + 1) * P], Vt[:, n, g * P:(g + 1) * P], wsT[:, g, :],
                                              start=True, stop=True)
                    mm.then_inc(sem["sv_done"], 1)

                pe.wait_ge(sem["wsT_done"], 1)
                pe.wait_ge(sem["ln_done"], 2)
                for g in range(4):
                    spatial(g)
                pe.wait_ge(sem["mod_fin"], jobs_taken(si) + 1)
                for c in range(KC):
                    pe.wait_ge(sem["xn_done"], U0[si] + 8 + c + 1)
                    down(2 * s.pB + c, (2 * s.pB + c) % SLOTS, LAT, xn_hi[:, c, 0:LAT], xn_lo[:, c, 0:LAT], c == 0, c == KC - 1)
                    if c < 4:
                        spatial(c + 4)
        for n in range(2):
            for k in range(KC):
                pe.wait_ge(sem["x_upd"], 8 * EV[6] + k + 1)
                mm = nc.tensor.transpose(out_rows(n)[:, k * P:(k + 1) * P], xT[:, k, n * P:(n + 1) * P], ident[:, :])
            mm.then_inc(sem["yt_done"], 1)


EV = {0: 1, 1: 2, 2: 3, 3: 4, 4: 5, 5: 6, 6: 7}
EV_BEFORE = {0: 0, 2: 2, 3: 3, 4: 4, 5: 5, 6: 6}
SQ_MMS = 5
Y0 = {1: 0, 2: 7, 3: 14, 4: 17, 5: 20, 6: 23, 7: 26}
NRM = {0: 0, 2: 1, 3: 2, 4: 3, 5: 4, 6: 5, 7: 6}
U0 = {0: 0, 1: 16, 2: 16, 3: 40, 4: 48, 5: 56, 6: 72}
X_BANKS = (1, 2, 3, 6)
DVE_PARAMS, DVE_LB = 2, 4
FIRST_SPLITS = (1, 3, 5, 6)
OUT_SPLITS = (1, 4, 6)
MIX_SPLITS = (4, 6, 7)
AB = 2


def jobs_taken(si):
    done = [j for i in JOBS_BEFORE if i <= si for j in JOBS_BEFORE[i]]
    done += [j for i in JOBS_AT if i <= si for _, jobs in JOBS_AT[i] for j in jobs]
    return max(done) + 1


def norm_units(T):
    return [(k, c) for k in range(KC) for c in range(T // LAT)]


def shift_of(mod_cols, layer, m, T):
    return [mod_cols(layer, c, m) for c in range(T // LAT)]


def raw_count(n, slot):
    return (n - slot) * (16 // SLOTS) + 16


def rows_of(xp, c):
    return xp[:, c, :].rearrange("p (r w) -> p r w", r=ROWS)[:, :, PAD:PAD + GRID_W]


def pool_windows(nc, dve, link, xp, xs, py, inv_cnt, sem):
    for c in range(POOL_TILES):
        cur, width = xp[:, c, :], 1
        n = ROWS * RW
        windows = ((2, 4), (8, 16))[c]
        for i in range(4):
            nxt = xs[:, i % 2, 0:n - width]
            link(nc.vector.tensor_tensor(nxt, cur[:, 0:n - width], cur[:, width:n], ALU.add))
            n -= width
            width *= 2
            cur = xs[:, i % 2, 0:n]
            if width in windows:
                half = windows.index(width)
                q = slice(64 * half, 64 * half + 64)
                start = PAD - width // 2
                full = bass.AP(xs, (i % 2) * ROWS * RW + start + 64 * half * 2 * ROWS * RW,
                               [[2 * ROWS * RW, 64], [RW, ROWS], [1, GRID_W]])
                cnt = bass.AP(inv_cnt, c * GRID_W + 64 * half * POOL_TILES * GRID_W,
                              [[POOL_TILES * GRID_W, 64], [0, ROWS], [1, GRID_W]])
                out = py[q, c, :].rearrange("p (r w) -> p r w", r=ROWS)
                link(nc.vector.tensor_tensor(out, full, cnt, ALU.mult))
                last = nc.vector.tensor_tensor(out, out, rows_of(xp, c)[q], ALU.subtract)
                link(last)
                if width == windows[1]:
                    break
    nc.vector.tensor_copy(py[:, 0, 0:1], py[:, 0, 0:1]).then_inc(sem["py_done"], 1)


def constants():
    i, j = np.arange(P)[:, None], np.arange(P)[None, :]
    masks = np.zeros((P, LEVELS, P), np.float32)
    masks[:, 0] = i == j
    for L in range(1, LEVELS):
        B = 1 << (L - 1)
        masks[:, L] = (i // (2 * B) == j // (2 * B)) & (i // B != j // B)
    inv = np.zeros((P, POOL_TILES, GRID_W), np.float32)
    pos = np.arange(GRID_W)
    for g, w in enumerate((2, 4, 8, 16)):
        lo, hi = np.clip(pos - w // 2, 0, GRID_W), np.clip(pos - w // 2 + w, 0, GRID_W)
        inv[64 * (g % 2):64 * (g % 2) + 64, g // 2] = 1.0 / (hi - lo)
    return {"ident": np.eye(P, dtype=np.float32), "masks": masks, "inv_cnt": inv}


def kernel(x, c, ctx, c_ctx, mod_w, mod_b, norm_g, ffn_w1, ffn_w3, ffn_w2, ab_w_in, pool_w, pool_scale,
           hgrn_lb, hgrn_norm_g, ab_w_out, gmlp_w_in, gmlp_ln_g, gmlp_ln_b, gmlp_w_s, gmlp_b_s,
           gmlp_w_out, final_g):
    import concourse.bacc as bacc
    from concourse.bass_utils import run_bass_kernel_spmd

    def flat(a, *shape):
        return np.ascontiguousarray(np.asarray(a).reshape(shape))

    params = np.concatenate([np.asarray(a).reshape(-1, P) for a in
                             (norm_g, hgrn_lb, hgrn_norm_g, pool_scale, c, c_ctx)])
    arrays = dict(
        x=flat(x, LAT, D), ctx=flat(ctx, CTX, D), params=params, mod_w=flat(mod_w, 2, D, N_MOD * D),
        mod_b=flat(mod_b, 2, N_MOD * D), w1=flat(ffn_w1, 2, 2, D, FF), w3=flat(ffn_w3, 2, 2, D, FF),
        w2=flat(ffn_w2, 2, 2, FF, D), ab_w_in=flat(ab_w_in, D, -1), pool_w=flat(pool_w, 4, 64, 64),
        ab_w_out=flat(ab_w_out, D, D), gmlp_w_in=flat(gmlp_w_in, D, 2 * D), gmlp_ln_g=flat(gmlp_ln_g, D),
        gmlp_ln_b=flat(gmlp_ln_b, D), gmlp_w_s=flat(gmlp_w_s, GROUPS, P, P), gmlp_b_s=flat(gmlp_b_s, D),
        gmlp_w_out=flat(gmlp_w_out, D, D), final_g=flat(final_g, D), **constants())
    nc = bacc.Bacc("TRN2", target_bir_lowering=False, num_devices=1)
    t = {}
    for name, a in arrays.items():
        t[name] = nc.dram_tensor(f"in_{name}", a.shape, mybir.dt.from_np(a.dtype), kind="ExternalInput").ap()
    t["out"] = nc.dram_tensor("out_y", (LAT, D), F32, kind="ExternalOutput").ap()
    build(nc, t)
    r = run_bass_kernel_spmd(nc, [{f"in_{k}": a for k, a in arrays.items()}], core_ids=[0])
    return r.results[0]["out_y"].reshape(1, LAT, D)
```
